# Optimizing a Trainium2 kernel written in Bass

```python
import jax, jax.numpy as jnp
from jax import lax
import numpy as np

D_MODEL = 1024
BATCH = 1
SEQ = 128
DEPTH = 1
DEC_BATCH = 1
DEC_SEQ = 512
PAST_LEN = 128

GRID_W = 64
CHUNK = GRID_W
N_HEADS = 4
HEAD_DIM = 256
D_MLSTM = N_HEADS * HEAD_DIM
N_FGROUPS = 4
FGROUP_DIM = 128
D_FOURIER = N_FGROUPS * FGROUP_DIM
N_EXPERTS = 16
N_EGROUPS = 4
EXPERTS_PER_GROUP = N_EXPERTS // N_EGROUPS
TOP_K = 2
D_EXPERT = 512
ALPHA = (2 * DEPTH) ** 0.25
BETA = (8 * DEPTH) ** -0.25
LN_EPS = 1e-6
SPLIT_POINTS = (D_MLSTM, 2 * D_MLSTM, 3 * D_MLSTM, 4 * D_MLSTM, 4 * D_MLSTM + D_FOURIER,
                4 * D_MLSTM + D_FOURIER + D_MODEL, 4 * D_MLSTM + D_FOURIER + 2 * D_MODEL)
GATE_OFFSET = 4 * D_MLSTM + D_FOURIER + 2 * D_MODEL
N_IN = GATE_OFFSET + 4 * N_HEADS

kernel_name = "mlstm_fnet_gated_moe_diffusion_step"

def layer_norm(x, g, b):
    xf = x.astype(jnp.float32)
    mu = jnp.mean(xf, axis=-1, keepdims=True)
    var = jnp.mean(jnp.square(xf - mu), axis=-1, keepdims=True)
    return ((xf - mu) * lax.rsqrt(var + LN_EPS) * g + b).astype(x.dtype)

def mlstm_scan(q, k, v, i_pre, log_f, C0, n0, m0):
    B, Hd, L, Dh = q.shape
    n_chunks = L // CHUNK

    def to_chunks(a):
        return jnp.moveaxis(a.reshape(B, Hd, n_chunks, CHUNK, *a.shape[3:]), 2, 0)

    causal = jnp.tril(jnp.ones((CHUNK, CHUNK), dtype=bool))

    def step(carry, xs):
        C, n, m = carry
        qc, kc, vc, ic, fc = xs
        b = jnp.cumsum(fc, axis=-1)
        log_d = jnp.where(causal, b[..., :, None] - b[..., None, :] + ic[..., None, :], -jnp.inf)
        log_inter = b + m[..., None]
        m_t = jnp.maximum(log_inter, jnp.max(log_d, axis=-1))
        s = jnp.einsum('bhtd,bhsd->bhts', qc, kc) * jnp.exp(log_d - m_t[..., None])
        w_inter = jnp.exp(log_inter - m_t)
        num = jnp.einsum('bhts,bhsd->bhtd', s, vc) + w_inter[..., None] * jnp.einsum('bhvk,bhtk->bhtv', C, qc)
        den = jnp.sum(s, axis=-1) + w_inter * jnp.einsum('bhk,bhtk->bht', n, qc)
        h = num / jnp.maximum(jnp.abs(den), jnp.exp(-m_t))[..., None]
        b_last = b[..., -1]
        log_w = b_last[..., None] - b + ic
        m_new = jnp.maximum(b_last + m, jnp.max(log_w, axis=-1))
        w = jnp.exp(log_w - m_new[..., None])
        decay = jnp.exp(b_last + m - m_new)
        C_new = decay[..., None, None] * C + jnp.einsum('bhsv,bhsk->bhvk', vc * w[..., None], kc)
        n_new = decay[..., None] * n + jnp.einsum('bhs,bhsk->bhk', w, kc)
        return (C_new, n_new, m_new), h

    xs = (to_chunks(q), to_chunks(k), to_chunks(v), to_chunks(i_pre), to_chunks(log_f))
    (C, n, m), h = lax.scan(step, (C0, n0, m0), xs)
    h = jnp.moveaxis(h, 0, 2).reshape(B, Hd, L, Dh)
    return h, (C, n, m)

def grouped_top2_moe(h, w_router, b_router, w_gate, w_up, w_down):
    probs = jax.nn.softmax((h @ w_router).astype(jnp.float32) + b_router, axis=-1)
    grp = probs.reshape(*probs.shape[:-1], N_EGROUPS, EXPERTS_PER_GROUP)
    top_v, top_i = lax.top_k(grp, TOP_K)
    best = jnp.argmax(jnp.sum(top_v, axis=-1), axis=-1)
    w = top_v / jnp.sum(top_v, axis=-1, keepdims=True)
    in_group = jnp.einsum('...gk,...gke->...ge', w, jax.nn.one_hot(top_i, EXPERTS_PER_GROUP, dtype=jnp.float32))
    combine = (jax.nn.one_hot(best, N_EGROUPS, dtype=jnp.float32)[..., None] * in_group)
    combine = combine.reshape(*probs.shape).astype(h.dtype)
    y = jnp.zeros_like(h)
    for e in range(N_EXPERTS):
        a = jax.nn.silu(h @ w_gate[e]) * (h @ w_up[e])
        y = y + combine[..., e:e + 1] * (a @ w_down[e])
    return y

def trunk_layer(x, mod, C0, n0, m0, w_in, b_in, w_a, w_b, w_out, g_head,
                ln1_g, ln1_b, ln2_g, ln2_b, w_router, b_router, w_gate, w_up, w_down):
    B, L, _ = x.shape
    shift1, scale1, gate1, shift2, scale2, gate2 = jnp.split(mod, 6, axis=-1)
    h = x * (1 + scale1) + shift1
    z = h @ w_in + b_in
    q, k, v, o, u, g_a, g_b, gates = jnp.split(z, SPLIT_POINTS, axis=-1)

    def heads(a):
        return a.astype(jnp.float32).reshape(B, L, N_HEADS, HEAD_DIM).transpose(0, 2, 1, 3)
    qh, kh, vh = heads(q), heads(k) * (HEAD_DIM ** -0.5), heads(v)
    gates = gates.astype(jnp.float32).reshape(B, L, 2, 2, N_HEADS).transpose(2, 3, 0, 4, 1)
    i_pre, log_f = gates[0], jax.nn.log_sigmoid(gates[1])

    def both(fwd, bwd):
        return jnp.concatenate([fwd, jnp.flip(bwd, axis=2)], axis=1)
    hs, state = mlstm_scan(both(qh, qh), both(kh, kh), both(vh, vh),
                           both(i_pre[0], i_pre[1]), both(log_f[0], log_f[1]), C0, n0, m0)
    hsum = (hs[:, :N_HEADS] + jnp.flip(hs[:, N_HEADS:], axis=2)).transpose(0, 2, 1, 3)
    mu = jnp.mean(hsum, axis=-1, keepdims=True)
    var = jnp.mean(jnp.square(hsum - mu), axis=-1, keepdims=True)
    hn = ((hsum - mu) * lax.rsqrt(var + LN_EPS)).reshape(B, L, D_MLSTM) * g_head
    y_a = (jax.nn.sigmoid(o.astype(jnp.float32)) * hn).astype(x.dtype) @ w_a

    uf = u.astype(jnp.float32).reshape(B, L, N_FGROUPS, FGROUP_DIM)
    y_f = jnp.real(jnp.fft.fft2(uf, axes=(1, 3), norm="ortho")).reshape(B, L, D_FOURIER).astype(x.dtype)
    y_b = y_f @ w_b

    merged = jax.nn.sigmoid(g_a) * y_a + jax.nn.sigmoid(g_b) * y_b
    x = layer_norm(ALPHA * x + gate1 * (merged @ w_out), ln1_g, ln1_b)

    h2 = x * (1 + scale2) + shift2
    y2 = grouped_top2_moe(h2, w_router, b_router, w_gate, w_up, w_down)
    x = layer_norm(ALPHA * x + gate2 * y2, ln2_g, ln2_b)
    return x, state

def setup_inputs(seed: int = 0) -> dict:
    key = jax.random.key(seed)
    ks = jax.random.split(key, 26)
    nrm = lambda k, shape, s: jax.random.normal(k, shape, jnp.float32) * s
    b_in = nrm(ks[8], (DEPTH, N_IN), 0.02)
    f_bias = jax.random.uniform(ks[9], (DEPTH, 2 * N_HEADS), jnp.float32, 3.0, 6.0)
    b_in = b_in.at[:, GATE_OFFSET + 2 * N_HEADS:].add(f_bias)
    return {
        "x_prompt": nrm(ks[0], (BATCH, SEQ, D_MODEL), 1.0),
        "x_sample": nrm(ks[1], (DEC_BATCH, DEC_SEQ, D_MODEL), 1.0),
        "state_C": nrm(ks[2], (DEC_BATCH, DEPTH, 2, N_HEADS, HEAD_DIM, HEAD_DIM), 0.1),
        "state_n": nrm(ks[3], (DEC_BATCH, DEPTH, 2, N_HEADS, HEAD_DIM), 0.1),
        "state_m": nrm(ks[4], (DEC_BATCH, DEPTH, 2, N_HEADS), 1.0),
        "c": nrm(ks[5], (DEC_BATCH, D_MODEL), 1.0),
        "c_ctx": nrm(ks[6], (D_MODEL,), 1.0),
        "w_in": nrm(ks[7], (DEPTH, D_MODEL, N_IN), D_MODEL ** -0.5),
        "b_in": b_in,
        "w_a": nrm(ks[10], (DEPTH, D_MLSTM, D_MODEL), D_MLSTM ** -0.5),
        "w_b": nrm(ks[11], (DEPTH, D_FOURIER, D_MODEL), D_FOURIER ** -0.5),
        "w_out": nrm(ks[12], (DEPTH, D_MODEL, D_MODEL), BETA * D_MODEL ** -0.5),
        "g_head": 1.0 + nrm(ks[13], (DEPTH, D_MLSTM), 0.02),
        "ln1_g": 1.0 + nrm(ks[14], (DEPTH, D_MODEL), 0.02),
        "ln1_b": nrm(ks[15], (DEPTH, D_MODEL), 0.02),
        "ln2_g": 1.0 + nrm(ks[16], (DEPTH, D_MODEL), 0.02),
        "ln2_b": nrm(ks[17], (DEPTH, D_MODEL), 0.02),
        "w_ada": nrm(ks[18], (DEPTH, D_MODEL, 6 * D_MODEL), 0.5 * D_MODEL ** -0.5),
        "b_ada": nrm(ks[19], (DEPTH, 6 * D_MODEL), 0.02),
        "w_router": nrm(ks[20], (D_MODEL, N_EXPERTS), D_MODEL ** -0.5),
        "b_router": nrm(ks[21], (N_EXPERTS,), 0.01),
        "w_gate": nrm(ks[22], (DEPTH, N_EXPERTS, D_MODEL, D_EXPERT), D_MODEL ** -0.5),
        "w_up": nrm(ks[23], (DEPTH, N_EXPERTS, D_MODEL, D_EXPERT), D_MODEL ** -0.5),
        "w_down": nrm(ks[24], (DEPTH, N_EXPERTS, D_EXPERT, D_MODEL), BETA * D_EXPERT ** -0.5),
    }

def reference(x_prompt, x_sample, state_C, state_n, state_m, c, c_ctx, w_in, b_in, w_a, w_b, w_out,
              g_head, ln1_g, ln1_b, ln2_g, ln2_b, w_ada, b_ada, w_router, b_router, w_gate, w_up, w_down):
    H2 = 2 * N_HEADS

    def layer_weights(l):
        return (w_in[l], b_in[l], w_a[l], w_b[l], w_out[l], g_head[l], ln1_g[l], ln1_b[l],
                ln2_g[l], ln2_b[l], w_router, b_router, w_gate[l], w_up[l], w_down[l])

    B = x_prompt.shape[0]
    C0 = jnp.zeros((B, H2, HEAD_DIM, HEAD_DIM), jnp.float32)
    n0 = jnp.zeros((B, H2, HEAD_DIM), jnp.float32)
    m0 = jnp.zeros((B, H2), jnp.float32)
    xp = x_prompt
    new_C, new_n, new_m = [], [], []
    for l in range(DEPTH):
        mod_ctx = (jax.nn.silu(c_ctx) @ w_ada[l] + b_ada[l]).reshape(1, 1, 6 * D_MODEL)
        xp, (C_l, n_l, m_l) = trunk_layer(xp, mod_ctx, C0, n0, m0, *layer_weights(l))
        new_C.append(C_l.reshape(B, 2, N_HEADS, HEAD_DIM, HEAD_DIM))
        new_n.append(n_l.reshape(B, 2, N_HEADS, HEAD_DIM))
        new_m.append(m_l.reshape(B, 2, N_HEADS))
    new_state_C = jnp.stack(new_C, axis=1).astype(x_prompt.dtype)
    new_state_n = jnp.stack(new_n, axis=1).astype(x_prompt.dtype)
    new_state_m = jnp.stack(new_m, axis=1).astype(x_prompt.dtype)

    Bd = x_sample.shape[0]
    xs = x_sample
    for l in range(DEPTH):
        mod_lat = (jax.nn.silu(c) @ w_ada[l] + b_ada[l])[:, None, :]
        Cl = state_C[:, l].reshape(Bd, H2, HEAD_DIM, HEAD_DIM).astype(jnp.float32)
        nl = state_n[:, l].reshape(Bd, H2, HEAD_DIM).astype(jnp.float32)
        ml = state_m[:, l].reshape(Bd, H2).astype(jnp.float32)
        xs, _ = trunk_layer(xs, mod_lat, Cl, nl, ml, *layer_weights(l))

    return (xp, xs, new_state_C, new_state_n, new_state_m)


_drawn_inputs = setup_inputs


def setup_inputs(seed=0):
    import zlib

    import numpy as np

    out = dict(_drawn_inputs(seed))
    spreads = {}
    factors = {'state_C': 8.0,
     'state_n': 8.0,
     'state_m': 8.0,
     'g_head': 46.721,
     'ln2_g': 23.254,
     'ln2_b': 23.386,
     'b_router': 19.143}
    for name, (base, spread) in spreads.items():
        noise = np.random.default_rng([zlib.crc32(name.encode()), seed]).standard_normal(out[name].shape)
        drawn = base * np.exp(spread * noise) if base else spread * noise
        out[name] = __import__('jax').numpy.asarray(drawn.astype(out[name].dtype))
    for name, factor in factors.items():
        out[name] = (out[name] * factor).astype(out[name].dtype)
    return out
```

```python
from contextlib import ExitStack

import numpy as np

import concourse.bass as bass
from concourse import mybir

F32 = mybir.dt.float32
I32 = mybir.dt.int32
ALU = mybir.AluOpType
ACT = mybir.ActivationFunctionType
AX = mybir.AxisListType.X

P = 128
D = 1024
KT = D // P
TL, TC = 512, 128
T = TL + TC
NT = T // P
NL = TL // P
H, HD = 4, 256
NZ = 52
ZQ, ZK, ZV, ZO, ZU, ZGA, ZGB = 0, 8, 16, 24, 32, 36, 44
GATE_OFF = NZ * P
NG, FD = 4, 128
E, EG, EPG = 16, 4, 4
DE = 512
SLOT_TILES = (2 * T + E * (P - 1)) // P
ROW_TILES = SLOT_TILES + 1
PAIRS = SLOT_TILES // 2
MIN_PAIRS = 2 * T // P // 2
ALPHA = 2.0 ** 0.25
EPS = 1e-6
NEG = -1.0e30
GR = 36
N_ADA = 6 * D // 512
N_ZB = NZ * P // 512


def dft_tables():
    a = 2 * np.pi * ((np.arange(P)[:, None] * np.arange(P)[None]) % P) / P
    t128 = np.concatenate([np.cos(a), -np.sin(a), np.sin(a)], 1) / np.sqrt(P)
    b = 2 * np.pi * ((np.arange(TL)[:, None] * np.arange(TL)[None]) % TL) / TL
    t512 = np.stack([np.cos(b), np.sin(b)]) / np.sqrt(TL)
    return t128.astype(np.float32), t512.astype(np.float32)


def build(nc, a):
    ctx = ExitStack()
    with ctx:
        def sb(name, shape, dt=F32):
            return ctx.enter_context(nc.sbuf_tensor(name, shape, dt))

        def pb(name):
            return ctx.enter_context(nc.psum_tensor(name, [P, 512], F32))

        def sem(name):
            return ctx.enter_context(nc.semaphore(name))

        mod_d = nc.dram_tensor("mod_d", (2, 6 * D), F32, kind="Internal").ap()
        h2_d = nc.dram_tensor("h2_d", (T, D), F32, kind="Internal").ap()
        slot_tok_d = nc.dram_tensor("slot_tok_d", (ROW_TILES * P, 1), I32, kind="Internal").ap()
        y_d = nc.dram_tensor("y_d", (SLOT_TILES * P, D), F32, kind="Internal").ap()

        z = sb("z", [P, NZ, T])
        r1 = sb("r1", [P, 5160])
        r2 = sb("r2", [P, 8192])
        r3 = sb("r3", [P, 5120])
        zf = z[:, :, :].rearrange("p f t -> p (f t)")

        ring = [r2[:, s * 4096:(s + 1) * 4096].rearrange("p (k n) -> p k n", k=KT) for s in range(2)]
        hT = r1[:, 0:KT * T].rearrange("p (k t) -> p k t", k=KT)
        x_sb = r3[:, :].rearrange("p (t d) -> p t d", t=NT)
        gate_i, gate_f, log_f, tmp_g, b_row, m_row = (r3[0:GR, n * T:(n + 1) * T] for n in range(6))
        zero_row = r3[0:GR, 6 * T:7 * T]
        bm_row = r3[0:GR, 7 * T:8 * T]
        mod = zf[0:2, 33280 - 12288:33280 - 6144]
        b_ada = zf[0:2, 33280 - 6144:33280]
        stack = zf[0:92, 0:P]
        wgate_raw = zf[:, 128:256].rearrange("p (k n) -> p k n", k=KT)
        wgate = zf[:, 256:1280].rearrange("p (k n) -> p k n", k=KT)
        zero_i = zf[0:ROW_TILES, 1280:1408].bitcast(I32)
        vaug = r1[:, 0:NT * H * 257].rearrange("p (t h v) -> p t h v", t=NT, h=H)
        c0_raw = r2[:, 0:4096].rearrange("p (j b k) -> p j b k", j=8, b=2)
        c0T = zf[:, ZV * T:ZV * T + 8 * 2 * 257].rearrange("p (j b v) -> p j b v", j=8, b=2)
        dp = [r2[:, s * 2048:(s + 1) * 2048].rearrange("p (s t) -> p s t", s=NL) for s in range(2)]
        qs = [r2[:, 4096 + s * 1024:4096 + (s + 1) * 1024].rearrange("p (b t) -> p b t", b=2) for s in range(2)]
        md = r2[:, 6144:6656]
        wq = r2[:, 6656:7168]
        ktok = r2[:, 7168:8192]
        dc = r2[:, 0:1024].rearrange("p (j t) -> p j t", j=8)
        mdc = r2[:, 2048:3072].rearrange("p (j t) -> p j t", j=8)
        c_out = [r2[:, 3072 + s * HD:3072 + (s + 1) * HD] for s in range(2)]
        n_out = [r2[0:1, 3584 + s * HD:3584 + (s + 1) * HD] for s in range(2)]
        wv = r2[:, 4096:6144].rearrange("p (j v) -> p j v", j=8)
        hsum = x_sb
        four_a = zf[:, 0:NT * NG * 256].rearrange("p (t g c f) -> p t g c f", t=NT, g=NG, c=2)
        four_l = zf[:, ZK * T:ZK * T + 4096].rearrange("p (c s t) -> p c s t", c=2, s=NL)
        t128_sb = zf[:, ZK * T + 4096:ZK * T + 4096 + 3 * P]
        wa_sb = r2[:, :].rearrange("p (k n) -> p k n", k=KT)
        wb_sb = r1[:, 0:4096].rearrange("p (k n) -> p k n", k=4)
        wo_sb = zf[:, 0:8192].rearrange("p (k n) -> p k n", k=KT)
        xr = r3[:, :].rearrange("p (t d) -> p t d", t=NT)
        rows1 = r2[:, :].rearrange("p (r d) -> p r d", r=8)
        G1L, G1C, S2L, S2C, H2L, H2C, LN1G, LN1B = range(8)
        h2 = r1[:, 0:5120].rearrange("p (t d) -> p t d", t=NT)
        h2T = [zf[:, 8192 + s * 1024:8192 + (s + 1) * 1024].rearrange("p (k t) -> p k t", k=KT) for s in range(2)]
        prob = r2[:, 0:80].rearrange("p (t e) -> p t e", t=NT)
        rt = r2[:, 80:560].rearrange("p (n t e) -> p n t e", n=6, t=NT)
        rs = r2[:, 560:800].rearrange("p (n g) -> p n g", n=12)
        cnt5 = r2[:, 800:880].rearrange("p (e t) -> p e t", e=E)
        est = r2[:, 880:944].rearrange("p (n e) -> p n e", n=4)
        own = r2[0:1, 944:944 + SLOT_TILES * E].rearrange("p (j e) -> p j e", e=E)
        slot_rows = r2[0:ROW_TILES, 1408:1536].bitcast(I32)
        slot_rows_f = r2[0:ROW_TILES, 1536:1664]
        wslot = [zf[:, s * 12288:(s + 1) * 12288] for s in range(2)]
        w_g = [w[:, 0:4096].rearrange("p (k n) -> p k n", k=KT) for w in wslot]
        w_u = [w[:, 4096:8192].rearrange("p (k n) -> p k n", k=KT) for w in wslot]
        w_d = [w[:, 8192:12288].rearrange("p (k n) -> p k n", k=4) for w in wslot]
        tail = zf[:, 24576:33280]
        hg = [tail[:, s * 1024:(s + 1) * 1024] for s in range(2)]
        hgT = [tail[:, 2048 + s * 1024:3072 + s * 1024] for s in range(2)]
        y_sb = [tail[:, 4096 + s * 1024:5120 + s * 1024] for s in range(2)]
        silu_g, act_a, act_aT = (tail[:, 6144 + n * 512:6656 + n * 512] for n in range(3))
        rows2 = r1[:, 0:4096].rearrange("p (r d) -> p r d", r=4)
        G2L, G2C, LN2G, LN2B = range(4)
        yg = [[r2[:, (s * 2 + k) * 1024:(s * 2 + k + 1) * 1024] for k in range(2)] for s in range(2)]

        ident = sb("ident", [P, P])
        mask_neg = sb("mask_neg", [P, 2, P])
        before = sb("before", [P, P])
        ones = sb("ones", [P, P])
        zeros = sb("zeros", [P, P])
        cols = sb("cols", [P, 92])
        cond = sb("cond", [P, 16])
        mcols = sb("mcols", [P, 16, 2])
        gbias = sb("gbias", [GR, 2])
        m0_col = sb("m0_col", [GR, 1])
        m0_bc = sb("m0_bc", [P, 8])
        neg_m = sb("neg_m", [GR, T])
        a_col = sb("a_col", [P, NT, GR])
        em_col = sb("em_col", [P, NT, GR])
        w_col = sb("w_col", [P, 8])
        den = sb("den", [P, 4])
        bn = sb("bn", [P, 20, 6])
        mv = sb("mv", [P, 20, 2])
        rstd = sb("rstd", [P, 20])
        wr_sb = sb("wr_sb", [P, KT, E])
        br_bc = sb("br_bc", [P, E])
        rev4 = sb("rev4", [P, EPG])
        thresh = sb("thresh", [P, NT])
        tile_no = sb("tile_no", [1, SLOT_TILES])
        own_f = sb("own_f", [1, SLOT_TILES])
        tile_expert = sb("tile_expert", [1, SLOT_TILES], I32)
        slot_f = sb("slot_f", [P, 2, NT])
        slot_i = sb("slot_i", [P, 2 * NT], I32)
        wtok = sb("wtok", [P, 2, NT])
        tok_id = sb("tok_id", [P, NT], I32)
        slot_tok = sb("slot_tok", [P, ROW_TILES], I32)
        n_tiles = sb("n_tiles", [1, 1], I32)
        half_tiles = sb("half_tiles", [1, 1], I32)
        tok_cell = [sb(f"tok_cell{s}", [P, 1], I32) for s in range(2)]

        bank = [pb(f"bank{n}") for n in range(8)]

        pool_setup = sem("pool_setup")
        stack_loaded = sem("stack_loaded")
        x_loaded = sem("x_loaded")
        bada_loaded = sem("bada_loaded")
        misc_loaded = sem("misc_loaded")
        ring_full = [sem(f"ring_full{s}") for s in range(2)]
        stack_turned = sem("stack_turned")
        cols_ready = sem("cols_ready")
        cond_ready = sem("cond_ready")
        ada_mm = sem("ada_mm")
        mod_ready = sem("mod_ready")
        mod_stored = sem("mod_stored")
        mod_turned = sem("mod_turned")
        mcols_ready = sem("mcols_ready")
        x_turned = sem("x_turned")
        hT_ready = sem("hT_ready")
        wgate_ready = sem("wgate_ready")
        gates_mm = sem("gates_mm")
        gates_out = sem("gates_out")
        z_mm = sem("z_mm")
        z_ctx_mm = sem("z_ctx_mm")
        z_out = sem("z_out")
        z_ctx_out = sem("z_ctx_out")
        act_chain = sem("act_chain")
        dve_chain = sem("dve_chain")
        pool_chain = sem("pool_chain")
        gate_exp = sem("gate_exp")
        gate_abs = sem("gate_abs")
        gate_rows = sem("gate_rows")
        gate_turned = sem("gate_turned")
        gate_cols = sem("gate_cols")
        v_turned = sem("v_turned")
        v_out = sem("v_out")
        v_out_dve = sem("v_out_dve")
        k_turned = sem("k_turned")
        k_out = sem("k_out")
        c0_loaded = sem("c0_loaded")
        c0_turned = sem("c0_turned")
        c0_out = sem("c0_out")
        n0_out = sem("n0_out")
        s_mm = sem("s_mm")
        m_mm = sem("m_mm")
        md_ready = sem("md_ready")
        d_ready = sem("d_ready")
        p_ready = sem("p_ready")
        unit_mm = sem("unit_mm")
        unit_out = sem("unit_out")
        ctx_mm = sem("ctx_mm")
        ctx_md = sem("ctx_md")
        ctx_d = sem("ctx_d")
        ctx_p = sem("ctx_p")
        ctx_num_mm = sem("ctx_num_mm")
        ctx_num_out = sem("ctx_num_out")
        state_mm = sem("state_mm")
        state_out = sem("state_out")
        state_stored = [sem(f"state_stored{s}") for s in range(2)]
        n_stored = [sem(f"n_stored{s}") for s in range(2)]
        small_stored = sem("small_stored")
        four_loaded = sem("four_loaded")
        four_a_mm = sem("four_a_mm")
        four_a_out = sem("four_a_out")
        four_mm = sem("four_mm")
        four_out = sem("four_out")
        sig_ready = sem("sig_ready")
        var_ready = sem("var_ready")
        std_ready = sem("std_ready")
        hn_ready = sem("hn_ready")
        hn_turned = sem("hn_turned")
        yin_ready = sem("yin_ready")
        wab_loaded = sem("wab_loaded")
        wo_loaded = sem("wo_loaded")
        y_mm = sem("y_mm")
        y_gated = sem("y_gated")
        merged = sem("merged")
        xr_loaded = sem("xr_loaded")
        rows1_loaded = sem("rows1_loaded")
        rows1_ready = sem("rows1_ready")
        o_mm = sem("o_mm")
        o_out = sem("o_out")
        ln_var = sem("ln_var")
        ln_std = sem("ln_std")
        xn_ready = sem("xn_ready")
        x1_ready = sem("x1_ready")
        h2_ready = sem("h2_ready")
        h2_stored = sem("h2_stored")
        h2_turned = sem("h2_turned")
        h2T_ready = sem("h2T_ready")
        logits_mm = sem("logits_mm")
        soft_in = sem("soft_in")
        soft_out = sem("soft_out")
        chosen = sem("chosen")
        rank_mm = sem("rank_mm")
        slots_ready = sem("slots_ready")
        zeros_stored = sem("zeros_stored")
        table_stored = sem("table_stored")
        table_loaded = sem("table_loaded")
        table_f = sem("table_f")
        table_turned = sem("table_turned")
        table_ready = sem("table_ready")
        wg_full = [sem(f"wg_full{s}") for s in range(2)]
        wu_full = [sem(f"wu_full{s}") for s in range(2)]
        wd_full = [sem(f"wd_full{s}") for s in range(2)]
        hg_full = [sem(f"hg_full{s}") for s in range(2)]
        cell_ready = sem("cell_ready")
        cell_seen = sem("cell_seen")
        hg_turned = sem("hg_turned")
        hgT_ready = sem("hgT_ready")
        gate_mm = sem("gate_mm")
        up_mm = sem("up_mm")
        silu_ready = sem("silu_ready")
        a_ready = sem("a_ready")
        a_turned = sem("a_turned")
        aT_ready = sem("aT_ready")
        down_mm = sem("down_mm")
        y_out = sem("y_out")
        zeros_ready = sem("zeros_ready")
        y_zeroed = sem("y_zeroed")
        y_stored = [sem(f"y_stored{s}") for s in range(2)]
        rows2_loaded = sem("rows2_loaded")
        yg_loaded = [sem(f"yg_loaded{s}") for s in range(2)]
        yg_free = sem("yg_free")
        fin_var = sem("fin_var")
        fin_std = sem("fin_std")
        out_ready = sem("out_ready")
        out_stored = [sem(f"out_stored{s}") for s in range(2)]

        def half_run(eng):
            eng.wait_ge(slots_ready, 1)
            return eng.value_load(half_tiles[0:1, 0:1], min_val=MIN_PAIRS, max_val=PAIRS)

        def gate_row(j):
            return j if j < 4 else 28 + j

        block = ctx.enter_context(nc.Block())

        @block.sync
        def _(sp):
            sp.dma_start(stack[0:8, :], a["c"].rearrange("b (k p) -> (b k) p", p=P)).then_inc(stack_loaded, 16)
            sp.dma_start(stack[8:16, :], a["c_ctx"].rearrange("(k p) -> k p", p=P)).then_inc(stack_loaded, 16)
            sp.dma_start(stack[16:68, :], a["b_in"][0, 0:GATE_OFF].rearrange("(k p) -> k p", p=P)).then_inc(stack_loaded, 16)
            sp.dma_start(stack[68:76, :], a["g_head"][0, :].rearrange("(k p) -> k p", p=P)).then_inc(stack_loaded, 16)
            sp.dma_start(stack[76:92, :], a["state_n"].rearrange("a b d h (k p) -> (a b d h k) p", p=P)).then_inc(stack_loaded, 16)

            def load_ring(src, col, s):
                sp.dma_start(ring[s], src[0, :, bass.ds(col, 512)].rearrange("(k p) n -> p k n", p=P)).then_inc(ring_full[s], 16)

            load_ring(a["w_ada"], 0, 0)
            load_ring(a["w_ada"], 512, 1)
            sp.dma_start(b_ada, a["b_ada"][0, :].partition_broadcast(2)).then_inc(bada_loaded, 16)
            sp.dma_start(x_sb[:, 0:NL, :], a["x_sample"][0].rearrange("(t p) d -> p t d", p=P)).then_inc(x_loaded, 16)
            sp.dma_start(x_sb[:, NL, :], a["x_prompt"][0]).then_inc(x_loaded, 16)
            with sp.Fori(1, N_ADA // 2) as i:
                for s in range(2):
                    sp.wait_ge(ada_mm, 2 * i + s - 1)
                    load_ring(a["w_ada"], 1024 * i + 512 * s, s)
            for s in range(2):
                sp.wait_ge(ada_mm, N_ADA - 1 + s)
                load_ring(a["w_in"], 512 * s, s)
            with sp.Fori(1, N_ZB // 2) as i:
                for s in range(2):
                    sp.wait_ge(z_ctx_mm, 2 * i + s - 1)
                    load_ring(a["w_in"], 1024 * i + 512 * s, s)
            sp.wait_ge(z_ctx_mm, N_ZB - 2)
            load_ring(a["w_in"], (N_ZB - 1) * 512, 0)
            sp.wait_ge(zeros_ready, 1)
            always = 2 * MIN_PAIRS + 1
            sp.dma_start(y_d[always * P:, :].rearrange("(p r) (c n) -> p (r c) n", p=P, n=P),
                         zeros[:, :].unsqueeze(1).to_broadcast([P, (SLOT_TILES - always) * KT, P])).then_inc(y_zeroed, 16)
            sp.wait_ge(z_ctx_mm, N_ZB)
            sp.dma_start(c0_raw, a["state_C"].rearrange("a b d h (v p) k -> p (a b d h) v k", p=P)).then_inc(c0_loaded, 16)
            sp.wait_ge(s_mm, H)
            sp.wait_ge(k_turned, 2)
            sp.dma_start(four_l, a["t512"].rearrange("c (s p) t -> p c s t", p=P)).then_inc(four_loaded, 16)
            sp.dma_start(t128_sb, a["t128"]).then_inc(four_loaded, 16)
            sp.wait_ge(unit_mm, 32)
            sp.dma_start(wb_sb, a["w_b"][0].rearrange("(k p) n -> p k n", p=P)).then_inc(wab_loaded, 16)
            sp.dma_start(wa_sb, a["w_a"][0].rearrange("(k p) n -> p k n", p=P)).then_inc(wab_loaded, 16)
            sp.wait_ge(four_mm, NG)
            sp.dma_start(wo_sb, a["w_out"][0].rearrange("(k p) n -> p k n", p=P)).then_inc(wo_loaded, 16)
            sp.wait_ge(hn_turned, 2 * KT)
            sp.dma_start(xr[:, 0:NL, :], a["x_sample"][0].rearrange("(t p) d -> p t d", p=P)).then_inc(xr_loaded, 16)
            sp.dma_start(xr[:, NL, :], a["x_prompt"][0]).then_inc(xr_loaded, 16)
            sp.wait_ge(y_mm, KT)
            sp.wait_ge(mod_stored, 16)
            for r, src in ((G1L, mod_d[0, 2 * D:3 * D]), (G1C, mod_d[1, 2 * D:3 * D]), (S2L, mod_d[0, 4 * D:5 * D]),
                           (S2C, mod_d[1, 4 * D:5 * D]), (H2L, mod_d[0, 3 * D:4 * D]), (H2C, mod_d[1, 3 * D:4 * D]),
                           (LN1G, a["ln1_g"][0, :]), (LN1B, a["ln1_b"][0, :])):
                sp.dma_start(rows1[:, r, :], src.partition_broadcast(P)).then_inc(rows1_loaded, 16)
            for tt in range(NT):
                sp.wait_ge(h2_ready, tt + 1)
                sp.dma_start(h2_d[tt * P:(tt + 1) * P, :], h2[:, tt, :]).then_inc(h2_stored, 16)
            sp.wait_ge(h2_stored, 16 * NT)
            sp.wait_ge(h2_turned, 2 * NT)
            for r, src in ((G2L, mod_d[0, 5 * D:6 * D]), (G2C, mod_d[1, 5 * D:6 * D]),
                           (LN2G, a["ln2_g"][0, :]), (LN2B, a["ln2_b"][0, :])):
                sp.dma_start(rows2[:, r, :], src.partition_broadcast(P)).then_inc(rows2_loaded, 16)
            sp.wait_ge(table_stored, 16 * 2 * NT)
            sp.dma_start(slot_rows[:, :], slot_tok_d.rearrange("(j p) o -> j (p o)", p=P)).then_inc(table_loaded, 16)
            sp.wait_ge(slots_ready, 1)
            sp.wait_ge(h2T_ready, 2 * NT)
            sp.wait_ge(logits_mm, NT)

            def load_expert(j, s):
                e = sp.value_load(tile_expert[0:1, bass.ds(j, 1)], min_val=0, max_val=E - 1)
                sp.dma_start(w_g[s], a["w_gate"][0][bass.ds(e, 1)].rearrange("e (k p) n -> p (e k) n", p=P)).then_inc(wg_full[s], 16)
                sp.dma_start(w_u[s], a["w_up"][0][bass.ds(e, 1)].rearrange("e (k p) n -> p (e k) n", p=P)).then_inc(wu_full[s], 16)
                return e

            def load_down(e, s):
                sp.dma_start(w_d[s], a["w_down"][0][bass.ds(e, 1)].rearrange("e (k p) n -> p (e k) n", p=P)).then_inc(wd_full[s], 16)

            half = half_run(sp)

            def load_tile(j, s):
                sp.wait_ge(up_mm, j - 1)
                e = load_expert(j, s)
                sp.wait_ge(down_mm, j - 1)
                load_down(e, s)

            load_down(load_expert(0, 0), 0)
            load_down(load_expert(1, 1), 1)
            load_tile(2, 0)
            with sp.Fori(1, PAIRS) as i:
                with sp.If(i < half):
                    load_tile(2 * i + 1, 1)
                    load_tile(2 * i + 2, 0)
            for tt in range(NT):
                sp.wait_ge(out_ready, tt + 1)
                dst = a["y_sample"][0, tt * P:(tt + 1) * P, :] if tt < NL else a["y_prompt"][0]
                sp.dma_start(dst, yg[tt % 2][0]).then_inc(out_stored[tt % 2], 16)
            sp.wait_ge(out_stored[0], 16 * 3)
            sp.wait_ge(out_stored[1], 16 * 2)
            sp.wait_ge(small_stored, 32)
            for s in range(2):
                sp.wait_ge(n_stored[s], 4 * 16)
                sp.wait_ge(state_stored[s], 8 * 16)

        @block.gpsimd
        def _(pool):
            chain = [0]

            def then(ins):
                chain[0] += 1
                ins.then_inc(pool_chain, 1)
                pool.wait_ge(pool_chain, chain[0])

            nc.gpsimd.dma_start(wgate_raw[:, :, :], a["w_in"][0, :, GATE_OFF:GATE_OFF + 16].rearrange("(k p) n -> p k n", p=P)).then_inc(misc_loaded, 16)
            then(nc.gpsimd.memset(gbias[:, :], 0.0))
            with nc.allow_non_contiguous_dma(reason="a few words"):
                for kind in range(2):
                    for d in range(2):
                        c = GATE_OFF + 8 * kind + 4 * d
                        nc.gpsimd.dma_start(gbias[32 * d:32 * d + 4, kind:kind + 1], a["b_in"][0, c:c + 4].rearrange("(h o) -> h o", o=1)).then_inc(misc_loaded, 16)
                for d in range(2):
                    nc.gpsimd.dma_start(m0_col[32 * d:32 * d + 4, :], a["state_m"][0, 0, d, :].rearrange("(h o) -> h o", o=1)).then_inc(misc_loaded, 16)
            nc.gpsimd.dma_start(m0_bc[:, :], a["state_m"].rearrange("a b d h -> (a b d h)").partition_broadcast(P)).then_inc(misc_loaded, 16)
            nc.gpsimd.dma_start(wr_sb[:, :, :], a["w_router"].rearrange("(k p) n -> p k n", p=P)).then_inc(misc_loaded, 16)
            nc.gpsimd.dma_start(br_bc[:, :], a["b_router"].partition_broadcast(P)).then_inc(misc_loaded, 16)
            then(nc.gpsimd.memset(ident[:, :], 0.0))
            nc.gpsimd.affine_select(out=ident[:, :], in_=ident[:, :], compare_op=ALU.not_equal, fill=1.0, base=0,
                                    pattern=[[-1, P]], channel_multiplier=1).then_inc(pool_setup, 1)
            nc.gpsimd.memset(ones[:, :], 1.0).then_inc(pool_setup, 1)
            nc.gpsimd.memset(zeros[:, :], 0.0).then_inc(zeros_ready, 1)
            then(nc.gpsimd.memset(mask_neg[:, :, :], 0.0))
            for d in range(2):
                m = mask_neg[:, d, :]
                sign = 1 if d == 0 else -1
                nc.gpsimd.affine_select(out=m, in_=m, compare_op=ALU.is_ge, fill=NEG, base=0,
                                        pattern=[[sign, P]], channel_multiplier=-sign).then_inc(pool_setup, 1)
            then(nc.gpsimd.memset(before[:, :], 1.0))
            nc.gpsimd.affine_select(out=before[:, :], in_=before[:, :], compare_op=ALU.is_gt, fill=0.0, base=0,
                                    pattern=[[1, P]], channel_multiplier=-1).then_inc(pool_setup, 1)
            nc.gpsimd.iota(tok_id[:, :], pattern=[[P, NT]], base=0, channel_multiplier=1).then_inc(pool_setup, 1)
            nc.gpsimd.memset(zero_i[:, :], 0).then_inc(pool_setup, 1)
            for i in range(EPG):
                then(nc.gpsimd.memset(rev4[:, i:i + 1], float(EPG - i)))
            for i in range(NT):
                then(nc.gpsimd.memset(thresh[:, i:i + 1], float(P * i)))
            nc.gpsimd.iota(tile_expert[:, :], pattern=[[1, SLOT_TILES]], base=0, channel_multiplier=0).then_inc(pool_setup, 1)
            pool.wait_ge(pool_setup, 8)
            nc.gpsimd.tensor_copy(tile_no[:, :], tile_expert[:, :]).then_inc(pool_setup, 1)
            nc.gpsimd.dma_start(slot_tok_d.rearrange("(j p) o -> j (p o)", p=P), zero_i[:, :]).then_inc(zeros_stored, 16)
            pool.wait_ge(pool_setup, 9)
            nc.gpsimd.memset(wgate[:, :, :], 0.0).then_inc(pool_setup, 1)
            pool.wait_ge(mod_ready, N_ADA)
            nc.gpsimd.dma_start(mod_d, mod).then_inc(mod_stored, 16)
            pool.wait_ge(gate_rows, 1)
            with nc.allow_non_contiguous_dma(reason="a few words"):
                nc.gpsimd.dma_start(a["new_m"][0, 0, 0, :].rearrange("(h o) -> h o", o=1), bm_row[0:4, T - 1:T]).then_inc(small_stored, 16)
                nc.gpsimd.dma_start(a["new_m"][0, 0, 1, :].rearrange("(h o) -> h o", o=1), bm_row[32:36, TL:TL + 1]).then_inc(small_stored, 16)
            for q in range(8):
                h, d = q // 2, q % 2
                for vb in range(2):
                    pool.wait_ge(state_out, 3 * q + vb + 1)
                    nc.gpsimd.dma_start(a["new_C"][0, 0, d, h, vb * P:(vb + 1) * P, :], c_out[vb]).then_inc(state_stored[vb], 16)
                pool.wait_ge(state_out, 3 * q + 3)
                nc.gpsimd.dma_start(a["new_n"][0, 0, d, h:h + 1, :], n_out[q % 2]).then_inc(n_stored[q % 2], 16)
            for m in range(KT):
                pool.wait_ge(y_gated, m + 1)
                nc.gpsimd.tensor_tensor(z[:, ZGA + m, :], z[:, ZGA + m, :], z[:, ZGB + m, :], ALU.add).then_inc(merged, 1)
            pool.wait_ge(rows1_ready, 1)
            for tt in range(NT):
                c = 0 if tt < NL else 1
                pool.wait_ge(xn_ready, tt + 1)
                then(nc.gpsimd.tensor_tensor(xr[:, tt, :], xr[:, tt, :], rows1[:, LN1G, :], ALU.mult))
                then(nc.gpsimd.tensor_tensor(xr[:, tt, :], xr[:, tt, :], rows1[:, LN1B, :], ALU.add))
                then(nc.gpsimd.tensor_tensor(h2[:, tt, :], xr[:, tt, :], rows1[:, S2L + c, :], ALU.mult))
                nc.gpsimd.tensor_tensor(h2[:, tt, :], h2[:, tt, :], rows1[:, H2L + c, :], ALU.add).then_inc(h2_ready, 1)
            pool.wait_ge(zeros_stored, 16)
            pool.wait_ge(slots_ready, 1)
            for n in range(2 * NT):
                nc.gpsimd.indirect_dma_start(slot_tok_d, bass.IndirectOffsetOnAxis(ap=slot_i[:, n:n + 1], axis=0),
                                             tok_id[:, n % NT:n % NT + 1], None).then_inc(table_stored, 16)
            pool.wait_ge(table_ready, 1)
            pool.wait_ge(h2_stored, 16 * NT)
            pool.wait_ge(logits_mm, NT)
            pool.wait_ge(merged, KT)
            pool.wait_ge(o_mm, 2 * NT)

            def gather(j, s):
                nc.gpsimd.tensor_copy(tok_cell[s][:, :], slot_tok[:, bass.ds(j, 1)]).then_inc(cell_ready, 1)
                pool.wait_ge(cell_ready, j + 1)
                pool.sem_inc(cell_seen, 1)
                nc.gpsimd.indirect_dma_start(hg[s], None, h2_d, bass.IndirectOffsetOnAxis(ap=tok_cell[s][:, :], axis=0)).then_inc(hg_full[s], 16)

            half = half_run(pool)
            gather(0, 0)
            gather(1, 1)
            with pool.Fori(1, PAIRS + 1) as i:
                with pool.If(i < half + 1):
                    for s in range(2):
                        pool.wait_ge(hg_full[s], 16 * i)
                        pool.wait_ge(hg_turned, 2 * i + s - 1)
                        gather(2 * i + s, s)
            pool.wait_ge(y_stored[0], 16 * half + 16)
            pool.wait_ge(y_stored[1], 16 * half)
            pool.sem_inc(cell_seen, 1)
            for tt in range(NT):
                if tt >= 2:
                    pool.wait_ge(out_stored[tt % 2], 16 * (tt // 2))
                for k in range(2):
                    nc.gpsimd.indirect_dma_start(yg[tt % 2][k], None, y_d, bass.IndirectOffsetOnAxis(ap=slot_i[:, k * NT + tt:k * NT + tt + 1], axis=0)).then_inc(yg_loaded[tt % 2], 16)

        @block.scalar
        def _(act):
            A = nc.scalar.activation
            chain = [0]

            def then(ins):
                chain[0] += 1
                ins.then_inc(act_chain, 1)
                act.wait_ge(act_chain, chain[0])

            act.wait_ge(cols_ready, 1)
            A(cond[:, :], cols[:, 0:16], ACT.Silu).then_inc(cond_ready, 1)
            act.wait_ge(mcols_ready, 1)
            act.wait_ge(mod_stored, 16)
            act.wait_ge(zeros_stored, 16)
            for k in range(KT):
                act.wait_ge(x_turned, k + 1)
                A(hT[:, k, 0:TL], bank[2 + k % 2][:, :], ACT.Identity, scale=mcols[:, 8 + k, 0:1], bias=mcols[:, k, 0:1])
                A(hT[:, k, TL:T], bank[4 + k % 2][:, 0:P], ACT.Identity, scale=mcols[:, 8 + k, 1:2], bias=mcols[:, k, 1:2]).then_inc(hT_ready, 1)
            act.wait_ge(gates_mm, 1)
            for n, dst in enumerate((gate_i, gate_f)):
                A(dst[:, 0:TL], bank[6][64 * n:64 * n + GR, :], ACT.Copy).then_inc(gates_out, 1)
                A(dst[:, TL:T], bank[7][64 * n:64 * n + GR, 0:P], ACT.Copy).then_inc(gates_out, 1)
            act.wait_ge(gate_abs, 1)
            then(A(tmp_g, tmp_g, ACT.Exp))
            A(tmp_g, tmp_g, ACT.Ln, bias=ones[0:GR, 0:1]).then_inc(gate_exp, 1)

            def z_block(b, par):
                for f in range(4):
                    act.wait_ge(z_mm, 4 * b + f + 1)
                    A(z[:, bass.ds(4 * b + f, 1), 0:TL].rearrange("p a t -> p (a t)"), bank[f][:, :], ACT.Identity,
                      bias=cols[:, bass.ds(16 + 4 * b + f, 1)]).then_inc(z_out, 1)

            with act.Fori(0, N_ZB // 2) as i:
                z_block(2 * i, 0)
                z_block(2 * i + 1, 1)
            z_block(N_ZB - 1, 0)
            act.wait_ge(gate_turned, 1)
            A(em_col[:, :, :], bank[7][:, 0:5 * GR].rearrange("p (t g) -> p t g", t=NT), ACT.Exp, scale=-1.0).then_inc(gate_cols, 1)
            for n in range(10):
                if n % 2 == 0:
                    act.wait_ge(v_turned, n + 1)
                    A(vaug[:, n // 2, 0:2, 0:HD], bank[n % 4][:, :].rearrange("p (h v) -> p h v", h=2), ACT.Copy).then_inc(v_out, 1)
            for n in range(2):
                act.wait_ge(k_turned, n + 1)
                A(ktok[:, n * 512:(n + 1) * 512], bank[4 + n][:, :], ACT.Copy, scale=HD ** -0.5).then_inc(k_out, 1)
            for j in range(8):
                act.wait_ge(c0_turned, j + 1)
                A(c0T[:, j, :, 0:HD], bank[j % 4][:, :].rearrange("p (b v) -> p b v", b=2), ACT.Copy).then_inc(c0_out, 1)

            def decay(q):
                h, d = q // 2, q % 2
                j = d * 4 + h
                r = gate_row(j)
                act.wait_ge(md_ready, q + 1)
                if q == 1:
                    for s in range(2):
                        act.wait_ge(state_stored[s], 8 * 16)
                        act.wait_ge(n_stored[s], 4 * 16)
                if q >= 2:
                    act.wait_ge(unit_mm, 4 * (q - 1))
                for s in range(NL):
                    A(dp[q % 2][:, s, s * P:(s + 1) * P], md[:, s * P:(s + 1) * P], ACT.Exp, bias=a_col[:, s, r:r + 1])
                    lo, hi = ((s + 1) * P, TL) if d == 0 else (0, s * P)
                    if hi > lo:
                        A(dp[q % 2][:, s, lo:hi], bank[4][:, lo:hi], ACT.Exp, bias=a_col[:, s, r:r + 1])
                if q >= 1:
                    act.wait_ge(p_ready, q)
                A(wq, bank[4][:, :], ACT.Exp, bias=m0_bc[:, j:j + 1]).then_inc(d_ready, 1)

            act.wait_ge(ctx_md, 1)
            for j in range(8):
                last = A(dc[:, j, :], mdc[:, j, :], ACT.Exp, bias=a_col[:, NL, gate_row(j):gate_row(j) + 1])
            last.then_inc(ctx_d, 1)
            for q in range(8):
                for vb in range(2):
                    act.wait_ge(state_mm, 3 * q + vb + 1)
                    if q >= 1:
                        act.wait_ge(state_stored[vb], 16 * q)
                    A(c_out[vb], bank[4 + vb][:, 0:HD], ACT.Copy).then_inc(state_out, 1)
                act.wait_ge(state_mm, 3 * q + 3)
                if q >= 2:
                    act.wait_ge(n_stored[q % 2], 16 * (q // 2))
                A(n_out[q % 2], bank[6][0:1, 0:HD], ACT.Copy).then_inc(state_out, 1)
            act.wait_ge(ctx_num_mm, 8)
            for q in range(8):
                decay(q)
            for f in (ZO, ZGA, ZGB):
                A(z[:, f:f + 8, :], z[:, f:f + 8, :], ACT.Sigmoid).then_inc(sig_ready, 1)
            for n in range(10):
                act.wait_ge(four_a_mm, n + 1)
                A(four_a[:, n // 2, 2 * (n % 2):2 * (n % 2) + 2].rearrange("p g c f -> p (g c f)"), bank[n % 2][:, :], ACT.Copy).then_inc(four_a_out, 1)
            for g in range(NG):
                act.wait_ge(four_mm, g + 1)
                A(z[:, ZU + g, 0:TL], bank[2 + g % 2][:, :], ACT.Copy)
                A(z[:, ZU + g, TL:T], bank[4 if g % 2 == 0 else 7][:, 0:P], ACT.Copy).then_inc(four_out, 1)
            act.wait_ge(var_ready, 1)
            A(rstd[:, :], rstd[:, :], ACT.Sqrt).then_inc(std_ready, 1)
            for tt in range(NT):
                act.wait_ge(ln_var, tt + 1)
                A(rstd[:, tt:tt + 1], rstd[:, tt:tt + 1], ACT.Sqrt).then_inc(ln_std, 1)
            for tt in range(NT):
                for n in range(2):
                    act.wait_ge(h2_turned, 2 * tt + n + 1)
                    if tt >= 2:
                        act.wait_ge(logits_mm, tt - 1)
                    A(h2T[tt % 2][:, 4 * n:4 * n + 4, :].rearrange("p k t -> p (k t)"), bank[2 + n][:, :], ACT.Copy).then_inc(h2T_ready, 1)
            act.wait_ge(soft_in, 1)
            A(prob[:, :, :], prob[:, :, :], ACT.Exp).then_inc(soft_out, 1)

            def silu(j):
                A(silu_g, bank[0][:, :], ACT.Silu).then_inc(silu_ready, 1)

            def store_y(j, half, s):
                act.wait_ge(down_mm, j + 1)
                A(y_sb[s][:, 0:512], bank[5][:, :], ACT.Copy).then_inc(y_out, 1)
                A(y_sb[s][:, 512:D], bank[6][:, :], ACT.Copy).then_inc(y_out, 1)
                act.wait_ge(y_out, 2 * j + 2)
                act.dma_start(y_d[bass.ds(P * j, P), :], y_sb[s]).then_inc(y_stored[s], 16)

            def step(j, before_half, s):
                act.wait_ge(gate_mm, j + 1)
                act.wait_ge(a_ready, j)
                silu(j)
                if not (isinstance(j, int) and j <= 2):
                    act.wait_ge(y_stored[1 - s], 16 * before_half)
                store_y(j - 1, before_half, 1 - s)

            half = half_run(act)
            act.wait_ge(y_zeroed, 16)
            act.wait_ge(gate_mm, 1)
            silu(0)
            step(1, 0, 1)
            step(2, 0, 0)
            with act.Fori(1, PAIRS) as i:
                with act.If(i < half):
                    step(2 * i + 1, i, 1)
                    step(2 * i + 2, i, 0)
            act.wait_ge(y_stored[0], 16 * half)
            store_y(2 * half, half, 0)
            for tt in range(NT):
                act.wait_ge(fin_var, tt + 1)
                A(rstd[:, tt:tt + 1], rstd[:, tt:tt + 1], ACT.Sqrt).then_inc(fin_std, 1)

        @block.tensor
        def _(pe):
            MM = nc.tensor.matmul

            def turn(out, in_, rows=P):
                return nc.tensor.transpose(out, in_, ident[0:rows, 0:rows])

            pe.wait_ge(pool_setup, 2)
            pe.wait_ge(stack_loaded, 80)
            turn(bank[7][:, 0:92], stack[:, :], 92).then_inc(stack_turned, 1)
            pe.wait_ge(cond_ready, 1)

            def ada_block(n, half, s):
                pe.wait_ge(ring_full[s], 16 * half + 16)
                for k in range(KT):
                    last = MM(bank[s][0:2, :], cond[:, k:k + 9:8], ring[s][:, k, :], start=(k == 0), stop=(k == KT - 1))
                last.then_inc(ada_mm, 1)

            for s in range(2):
                ada_block(s, 0, s)
            with pe.Fori(1, N_ADA // 2) as i:
                for s in range(2):
                    pe.wait_ge(mod_ready, 2 * i + s - 1)
                    ada_block(2 * i + s, i, s)
            pe.wait_ge(mod_ready, 4)
            for n in range(16):
                last = turn(bank[6][:, 2 * n:2 * n + 2], mod[:, n * P:(n + 1) * P], 2)
            last.then_inc(mod_turned, 1)
            pe.wait_ge(x_loaded, 32)
            for k in range(KT):
                if k >= 2:
                    pe.wait_ge(hT_ready, k - 1)
                for tt in range(NL):
                    turn(bank[2 + k % 2][:, tt * P:(tt + 1) * P], x_sb[:, tt, k * P:(k + 1) * P])
                turn(bank[4 + k % 2][:, 0:P], x_sb[:, NL, k * P:(k + 1) * P]).then_inc(x_turned, 1)
            pe.wait_ge(wgate_ready, 1)
            for k in range(KT):
                pe.wait_ge(hT_ready, k + 1)
                MM(bank[6][:, :], wgate[:, k, :], hT[:, k, 0:TL], start=(k == 0), stop=(k == KT - 1))
                last = MM(bank[7][:, 0:P], wgate[:, k, :], hT[:, k, TL:T], start=(k == 0), stop=(k == KT - 1))
            last.then_inc(gates_mm, 1)

            def z_block(b, full, s, first=False):
                pe.wait_ge(ring_full[s], 16 * full)
                for f in range(4):
                    if not first:
                        pe.wait_ge(z_out, 4 * b + f - 3)
                    for k in range(KT):
                        last = MM(bank[f][:, :], ring[s][:, k, f * P:(f + 1) * P], hT[:, k, 0:TL], start=(k == 0), stop=(k == KT - 1))
                    last.then_inc(z_mm, 1)
                    if f == 0 and not first:
                        pe.wait_ge(z_ctx_out, b)
                    for k in range(KT):
                        last = MM(bank[4][:, f * P:(f + 1) * P], ring[s][:, k, f * P:(f + 1) * P], hT[:, k, TL:T], start=(k == 0), stop=(k == KT - 1))
                last.then_inc(z_ctx_mm, 1)

            pe.wait_ge(mod_ready, N_ADA)
            z_block(0, N_ADA // 2 + 1, 0, first=True)
            z_block(1, N_ADA // 2 + 1, 1)
            with pe.Fori(1, N_ZB // 2) as i:
                z_block(2 * i, N_ADA // 2 + 1 + i, 0)
                z_block(2 * i + 1, N_ADA // 2 + 1 + i, 1)
            z_block(N_ZB - 1, N_ADA // 2 + 1 + N_ZB // 2, 0)
            pe.wait_ge(gate_rows, 1)
            for n in range(2 * NT):
                src = (gate_i, bm_row)[n // NT]
                last = turn(bank[6 + n // NT][:, (n % NT) * GR:(n % NT + 1) * GR], src[:, (n % NT) * P:(n % NT + 1) * P], GR)
            last.then_inc(gate_turned, 1)
            pe.wait_ge(z_out, NZ)
            pe.wait_ge(z_ctx_out, N_ZB)
            for n in range(2 * NT):
                if n >= 4:
                    pe.wait_ge(v_out if n % 2 == 0 else v_out_dve, (n - 4) // 2 + 1)
                for f in range(4):
                    last = turn(bank[n % 4][:, f * P:(f + 1) * P], z[:, ZV + 4 * (n % 2) + f, (n // 2) * P:(n // 2 + 1) * P])
                last.then_inc(v_turned, 1)
            for n in range(2):
                for f in range(4):
                    last = turn(bank[4 + n][:, f * P:(f + 1) * P], z[:, ZK + 4 * n + f, TL:T])
                last.then_inc(k_turned, 1)
            pe.wait_ge(c0_loaded, 16)
            pe.wait_ge(v_out, 5)
            pe.wait_ge(v_out_dve, 5)
            for j in range(8):
                if j >= 4:
                    pe.wait_ge(c0_out, j - 3)
                for kb in range(2):
                    for vb in range(2):
                        last = turn(bank[j % 4][:, (2 * kb + vb) * P:(2 * kb + vb + 1) * P], c0_raw[:, j, vb, kb * P:(kb + 1) * P])
                last.then_inc(c0_turned, 1)
            pe.wait_ge(c0_out, 8)
            pe.wait_ge(n0_out, 1)
            pe.wait_ge(k_out, 2)
            pe.wait_ge(gate_cols, 2)

            def minus_m(dst, j, lo, hi):
                r = gate_row(j)
                return MM(dst, ident[0:GR, r:r + 1].to_broadcast([GR, P]), neg_m[:, lo:hi], start=True, stop=True)

            for h in range(H):
                for b in range(2):
                    MM(bank[0][:, h * P:(h + 1) * P], z[:, ZK + 2 * h + b, TL:T], z[:, ZQ + 2 * h + b, TL:T], start=(b == 0), stop=(b == 1))
            for j in range(8):
                last = minus_m(bank[1 + j // 4][:, (j % 4) * P:(j % 4 + 1) * P], j, TL, T)
            last.then_inc(ctx_mm, 1)
            pe.wait_ge(ctx_p, 1)
            for q in range(8):
                h, d = q // 2, q % 2
                j = d * 4 + h
                if q >= 1:
                    pe.wait_ge(ctx_num_out, q)
                MM(bank[3][:, 0:257], dc[:, j, :], vaug[:, NL, h, :], start=True, stop=True).then_inc(ctx_num_mm, 1)
                for vb in range(2):
                    if q >= 1:
                        pe.wait_ge(state_out, 3 * q - 2 + vb)
                    MM(bank[4 + vb][:, 0:HD], wv[:, j, vb * P:(vb + 1) * P], ktok[:, h * HD:(h + 1) * HD], start=True, stop=True).then_inc(state_mm, 1)
                if q >= 1:
                    pe.wait_ge(state_out, 3 * q)
                MM(bank[6][0:1, 0:HD], w_col[:, j:j + 1], ktok[:, h * HD:(h + 1) * HD], start=True, stop=True).then_inc(state_mm, 1)
            pe.wait_ge(ctx_num_out, 8)
            pe.wait_ge(state_out, 24)

            def scores(h):
                for s in range(NL):
                    for b in range(2):
                        last = MM(bank[s][:, :], z[:, ZK + 2 * h + b, s * P:(s + 1) * P], z[:, ZQ + 2 * h + b, 0:TL], start=(b == 0), stop=(b == 1))
                last.then_inc(s_mm, 1)

            def maxima(q):
                if q >= 1:
                    pe.wait_ge(d_ready, q)
                minus_m(bank[4][:, :], (q % 2) * 4 + q // 2, 0, TL).then_inc(m_mm, 1)

            def units(q):
                h, d = q // 2, q % 2
                j = d * 4 + h
                dec = dp[q % 2]
                for tt in range(NL):
                    u = 4 * q + tt
                    if u >= 3:
                        pe.wait_ge(unit_out, u - 2)
                    dst = bank[5 + u % 3][:, 0:257]
                    for n, s in enumerate(range(tt + 1) if d == 0 else range(tt, NL)):
                        MM(dst, dec[:, s, tt * P:(tt + 1) * P], vaug[:, s, h, :], start=(n == 0), stop=False)
                    for b in range(2):
                        last = MM(dst, qs[q % 2][:, b, tt * P:(tt + 1) * P], c0T[:, j, b, :], start=False, stop=(b == 1))
                    last.then_inc(unit_mm, 1)

            scores(0)
            maxima(0)
            for q in range(8):
                if q + 1 < 8 and q % 2 == 0:
                    maxima(q + 1)
                pe.wait_ge(p_ready, q + 1)
                if q % 2 == 1 and q + 1 < 8:
                    scores(q // 2 + 1)
                    maxima(q + 1)
                units(q)
            pe.wait_ge(unit_out, 32)
            pe.wait_ge(four_loaded, 32)
            for n in range(10):
                if n >= 2:
                    pe.wait_ge(four_a_out, n - 1)
                for g in range(2):
                    last = MM(bank[n % 2][:, g * 256:(g + 1) * 256], z[:, ZU + 2 * (n % 2) + g, (n // 2) * P:(n // 2 + 1) * P], t128_sb[:, 0:256], start=True, stop=True)
                last.then_inc(four_a_mm, 1)
            pe.wait_ge(four_a_out, 10)
            for g in range(NG):
                if g >= 2:
                    pe.wait_ge(four_out, g - 1)
                for s in range(NL):
                    for c in range(2):
                        MM(bank[2 + g % 2][:, :], four_a[:, s, g, c, :], four_l[:, c, s, :], start=(s + c == 0), stop=(s == NL - 1 and c == 1))
                ctx_bank = bank[4 if g % 2 == 0 else 7]
                for c in range(2):
                    last = MM(ctx_bank[:, 0:P], four_a[:, NL, g, c, :], t128_sb[:, 256 * c:256 * c + P], start=(c == 0), stop=(c == 1))
                last.then_inc(four_mm, 1)
            pe.wait_ge(four_out, NG)
            TB = ((6, 7), (4, 5))
            for k in range(KT):
                pe.wait_ge(hn_ready, 1)
                if k >= 2:
                    pe.wait_ge(yin_ready, k - 1)
                for tt in range(NL):
                    last = turn(bank[TB[k % 2][0]][:, tt * P:(tt + 1) * P], hsum[:, tt, k * P:(k + 1) * P])
                last.then_inc(hn_turned, 1)
                turn(bank[TB[k % 2][1]][:, 0:P], hsum[:, NL, k * P:(k + 1) * P]).then_inc(hn_turned, 1)
            pe.wait_ge(wab_loaded, 32)
            YB = ((0, 1, 2), (3, 4, 5))
            for m in range(KT):
                ba, bc, bb = YB[m % 2]
                if m == 0:
                    pe.wait_ge(yin_ready, KT)
                if m >= 2:
                    pe.wait_ge(y_gated, m - 1)
                for w, base, kt, dst, off in ((wa_sb, ZO, KT, ba, 0), (wb_sb, ZU, 4, bb, P)):
                    for k in range(kt):
                        MM(bank[dst][:, :], w[:, k, m * P:(m + 1) * P], z[:, base + k, 0:TL], start=(k == 0), stop=(k == kt - 1))
                    for k in range(kt):
                        last = MM(bank[bc][:, off:off + P], w[:, k, m * P:(m + 1) * P], z[:, base + k, TL:T], start=(k == 0), stop=(k == kt - 1))
                last.then_inc(y_mm, 1)
            pe.wait_ge(wo_loaded, 16)
            OB = ((6, 7), (0, 1))
            pe.wait_ge(merged, KT)
            for tt in range(NT):
                if tt >= 2:
                    pe.wait_ge(o_out, tt - 1)
                for n in range(2):
                    for k in range(KT):
                        last = MM(bank[OB[tt % 2][n]][:, :], z[:, ZGA + k, tt * P:(tt + 1) * P], wo_sb[:, k, n * 512:(n + 1) * 512], start=(k == 0), stop=(k == KT - 1))
                    last.then_inc(o_mm, 1)

            def router(tt):
                for k in range(KT):
                    pe.wait_ge(h2T_ready, 2 * tt + k // 4 + 1)
                    last = MM(bank[4][:, tt * E:(tt + 1) * E], h2T[tt % 2][:, k, :], wr_sb[:, k, :], start=(k == 0), stop=(k == KT - 1))
                last.then_inc(logits_mm, 1)

            for tt in range(NT):
                pe.wait_ge(h2_ready, tt + 1)
                for n in range(2):
                    if tt >= 1:
                        pe.wait_ge(h2T_ready, 2 * tt - 1 + n)
                    for k in range(4):
                        last = turn(bank[2 + n][:, k * P:(k + 1) * P], h2[:, tt, (4 * n + k) * P:(4 * n + k + 1) * P])
                    last.then_inc(h2_turned, 1)
                router(tt)
            pe.wait_ge(chosen, 1)
            for tt in range(NT):
                for s in range(tt):
                    MM(bank[5][:, tt * E:(tt + 1) * E], ones[:, :], rt[:, 5, s, :], start=(s == 0), stop=False)
                MM(bank[5][:, tt * E:(tt + 1) * E], before[:, :], rt[:, 5, tt, :], start=(tt == 0), stop=True)
            for s in range(NT):
                last = MM(bank[5][:, NT * E:(NT + 1) * E], ones[:, :], rt[:, 5, s, :], start=(s == 0), stop=(s == NT - 1))
            last.then_inc(rank_mm, 1)
            pe.wait_ge(table_f, 1)
            turn(bank[7][:, 0:ROW_TILES], slot_rows_f[:, :], ROW_TILES).then_inc(table_turned, 1)

            def turn_rows(j, full, s):
                pe.wait_ge(hg_full[s], 16 * full)
                for n in range(2):
                    for k in range(4):
                        last = turn(bank[2 + n][:, k * P:(k + 1) * P], hg[s][:, (4 * n + k) * P:(4 * n + k + 1) * P])
                last.then_inc(hg_turned, 1)

            def project(dst, w, s):
                for k in range(KT):
                    last = MM(dst[:, :], hgT[s][:, k * P:(k + 1) * P], w[s][:, k, :], start=(k == 0), stop=(k == KT - 1))
                return last

            def turn_a():
                for f in range(4):
                    last = turn(bank[4][:, f * P:(f + 1) * P], act_a[:, f * P:(f + 1) * P])
                last.then_inc(a_turned, 1)

            def down(s):
                for n in range(2):
                    for f in range(4):
                        last = MM(bank[5 + n][:, :], act_aT[:, f * P:(f + 1) * P], w_d[s][:, f, n * 512:(n + 1) * 512], start=(f == 0), stop=(f == 3))
                last.then_inc(down_mm, 1)

            def moe_step(j, full, s, prev_full, y_free=True):
                pe.wait_ge(hgT_ready, j + 1)
                pe.wait_ge(wg_full[s], 16 * full)
                pe.wait_ge(silu_ready, j)
                project(bank[0], w_g, s).then_inc(gate_mm, 1)
                pe.wait_ge(a_ready, j)
                turn_a()
                pe.wait_ge(wu_full[s], 16 * full)
                project(bank[1], w_u, s).then_inc(up_mm, 1)
                pe.wait_ge(aT_ready, j)
                pe.wait_ge(wd_full[1 - s], 16 * prev_full)
                if y_free:
                    pe.wait_ge(y_out, 2 * j - 2)
                down(1 - s)
                turn_rows(j + 1, prev_full + 1, 1 - s)

            half = half_run(pe)
            turn_rows(0, 1, 0)
            pe.wait_ge(hgT_ready, 1)
            turn_rows(1, 1, 1)
            pe.wait_ge(wg_full[0], 16)
            project(bank[0], w_g, 0).then_inc(gate_mm, 1)
            pe.wait_ge(wu_full[0], 16)
            project(bank[1], w_u, 0).then_inc(up_mm, 1)
            moe_step(1, 1, 1, 1, y_free=False)
            moe_step(2, 2, 0, 1)
            with pe.Fori(1, PAIRS) as i:
                with pe.If(i < half):
                    moe_step(2 * i + 1, i + 1, 1, i + 1)
                    moe_step(2 * i + 2, i + 2, 0, i + 1)
            pe.wait_ge(a_ready, 2 * half + 1)
            turn_a()
            pe.wait_ge(aT_ready, 2 * half + 1)
            pe.wait_ge(wd_full[0], 16 * half + 16)
            pe.wait_ge(y_out, 4 * half)
            down(0)

        @block.vector
        def _(dve):
            V = nc.vector
            chain = [0]

            def then(ins):
                chain[0] += 1
                ins.then_inc(dve_chain, 1)
                dve.wait_ge(dve_chain, chain[0])

            dve.wait_ge(stack_turned, 1)
            V.tensor_copy(cols[:, :], bank[7][:, 0:92]).then_inc(cols_ready, 1)
            dve.wait_ge(pool_setup, 10)
            dve.wait_ge(misc_loaded, 16 * 10)
            V.tensor_copy(wgate[:, :, :].rearrange("p k (g c) -> p k g c", g=4)[:, :, :, 0:4],
                          wgate_raw[:, :, :].rearrange("p k (g c) -> p k g c", g=4)).then_inc(wgate_ready, 1)
            dve.wait_ge(bada_loaded, 16)

            def mod_block(n, s):
                dve.wait_ge(ada_mm, n + 1)
                V.tensor_tensor(mod[:, bass.ds(512 * n, 512)], bank[s][0:2, :], b_ada[:, bass.ds(512 * n, 512)], ALU.add).then_inc(mod_ready, 1)

            with dve.Fori(0, N_ADA // 2) as i:
                for s in range(2):
                    mod_block(2 * i + s, s)
            dve.wait_ge(mod_turned, 1)
            turned = bank[6][:, 0:32].rearrange("p (n c) -> p n c", c=2)
            V.tensor_copy(mcols[:, 0:8, :], turned[:, 0:8, :]).then_inc(dve_chain, 1)
            V.tensor_scalar_add(mcols[:, 8:16, :], turned[:, 8:16, :], 1.0).then_inc(mcols_ready, 1)
            chain[0] += 1
            dve.wait_ge(gates_out, 4)
            V.tensor_scalar(gate_i, gate_i, gbias[:, 0:1], None, ALU.add).then_inc(dve_chain, 1)
            V.memset(zero_row, 0.0).then_inc(dve_chain, 1)
            V.memset(b_row, 0.0).then_inc(dve_chain, 1)
            V.memset(m_row, 0.0).then_inc(dve_chain, 1)
            chain[0] += 4
            then(V.tensor_scalar(gate_f, gate_f, gbias[:, 1:2], None, ALU.add))
            V.scalar_tensor_tensor(out=tmp_g, in0=gate_f, scalar=-1.0, in1=gate_f, op0=ALU.mult, op1=ALU.min).then_inc(gate_abs, 1)

            def gate_stage():
                dve.wait_ge(gate_exp, 1)
                then(V.scalar_tensor_tensor(out=log_f, in0=gate_f, scalar=0.0, in1=tmp_g, op0=ALU.min, op1=ALU.subtract))
                spans = []
                for lo, hi in ((0, TL), (TL, T)):
                    spans.append((slice(0, 4), slice(lo, hi), lo))
                    spans.append((slice(32, 36), slice(hi - 1, lo - 1 if lo else None, -1), lo))
                for r, t, lo in spans:
                    last = V.tensor_tensor_scan(b_row[r, t], log_f[r, t], zero_row[r, t], 0.0, ALU.add, ALU.add)
                then(last)
                then(V.tensor_tensor(gate_i, gate_i, b_row, ALU.subtract))
                for r, t, lo in spans:
                    init = m0_col[r, 0:1] if lo == 0 else 0.0
                    last = V.tensor_tensor_scan(m_row[r, t], gate_i[r, t], gate_i[r, t], init, ALU.max, ALU.max)
                then(last)
                then(V.tensor_tensor(bm_row, b_row, m_row, ALU.add))
                V.tensor_scalar_mul(neg_m[:, :], m_row, -1.0).then_inc(gate_rows, 1)

            def z_block(b, par):
                dve.wait_ge(z_ctx_mm, b + 1)
                V.tensor_tensor(z[:, bass.ds(4 * b, 4), TL:T], bank[4][:, :].rearrange("p (f t) -> p f t", f=4),
                                cols[:, bass.ds(16 + 4 * b, 4)].unsqueeze(2).to_broadcast([P, 4, P]), ALU.add).then_inc(z_ctx_out, 1)

            dve.wait_ge(mod_stored, 16)
            dve.wait_ge(zeros_stored, 16)
            z_block(0, 0)
            gate_stage()
            with dve.Fori(1, N_ZB) as i:
                z_block(i, 0)
            dve.wait_ge(gate_turned, 1)
            V.tensor_copy(a_col[:, :, :], bank[6][:, 0:5 * GR].rearrange("p (t g) -> p t g", t=NT)).then_inc(gate_cols, 1)
            V.memset(vaug[:, :, :, HD:HD + 1], 1.0).then_inc(dve_chain, 1)
            chain[0] += 1
            for n in range(1, 10, 2):
                dve.wait_ge(v_turned, n + 1)
                V.tensor_copy(vaug[:, n // 2, 2:4, 0:HD], bank[n % 4][:, :].rearrange("p (h v) -> p h v", h=2)).then_inc(v_out_dve, 1)
            V.tensor_copy(c0T[:, :, :, HD:HD + 1], cols[:, 76:92].rearrange("p (j b o) -> p j b o", j=8, b=2)).then_inc(n0_out, 1)

            def masked(q):
                d = q % 2
                dve.wait_ge(m_mm, q + 1)
                V.tensor_tensor(md.rearrange("p (b t) -> p b t", b=NL), bank[4][:, :].rearrange("p (b t) -> p b t", b=NL),
                                mask_neg[:, d, :].unsqueeze(1).to_broadcast([P, NL, P]), ALU.add).then_inc(md_ready, 1)

            def weighted(q):
                h, d = q // 2, q % 2
                dec = dp[q % 2]
                dve.wait_ge(d_ready, q + 1)
                dve.wait_ge(s_mm, h + 1)
                for b in range(2):
                    V.tensor_tensor(qs[q % 2][:, b, :], z[:, ZQ + 2 * h + b, 0:TL], wq, ALU.mult)
                for s in range(NL):
                    lo, hi = (s * P, TL) if d == 0 else (0, (s + 1) * P)
                    last = V.scalar_tensor_tensor(out=dec[:, s, lo:hi], in0=bank[s][:, lo:hi], scalar=HD ** -0.5, in1=dec[:, s, lo:hi], op0=ALU.mult, op1=ALU.mult)
                last.then_inc(p_ready, 1)

            def finish_rows(num, n, tt, h, d, out_sem):
                r = gate_row(d * 4 + h)
                low = den[:, 2 * (n % 2):2 * (n % 2) + 1]
                inv = den[:, 2 * (n % 2) + 1:2 * (n % 2) + 2]
                then(V.tensor_scalar(low, num[:, HD:HD + 1], -1.0, em_col[:, tt, r:r + 1], ALU.mult, ALU.max))
                then(V.tensor_tensor(low, low, num[:, HD:HD + 1], ALU.max))
                then(V.reciprocal(inv, low))
                out = hsum[:, tt, h * HD:(h + 1) * HD]
                if d == 0:
                    V.tensor_scalar(out, num[:, 0:HD], inv, None, ALU.mult).then_inc(out_sem, 1)
                else:
                    V.scalar_tensor_tensor(out=out, in0=num[:, 0:HD], scalar=inv, in1=out, op0=ALU.mult, op1=ALU.add).then_inc(out_sem, 1)

            def consume(q):
                for tt in range(NL):
                    u = 4 * q + tt
                    dve.wait_ge(unit_mm, u + 1)
                    finish_rows(bank[5 + u % 3], u, tt, q // 2, q % 2, unit_out)

            dve.wait_ge(gate_cols, 2)
            dve.wait_ge(small_stored, 32)
            dve.wait_ge(ctx_mm, 1)
            for d in range(2):
                last = V.tensor_tensor(mdc[:, 4 * d:4 * d + 4, :], bank[1 + d][:, :].rearrange("p (j t) -> p j t", j=4),
                                       mask_neg[:, d, :].unsqueeze(1).to_broadcast([P, 4, P]), ALU.add)
            last.then_inc(ctx_md, 1)
            dve.wait_ge(ctx_d, 1)
            V.tensor_copy(w_col[:, 0:4], dc[:, 0:4, P - 1])
            then(V.tensor_copy(w_col[:, 4:8], dc[:, 4:8, 0]))
            for j in range(8):
                V.tensor_scalar(wv[:, j, :], vaug[:, NL, j % 4, 0:HD], w_col[:, j:j + 1], None, ALU.mult)
            for d in range(2):
                part = dc[:, 4 * d:4 * d + 4, :]
                last = V.scalar_tensor_tensor(out=part, in0=bank[0][:, :].rearrange("p (j t) -> p j t", j=4), scalar=HD ** -0.5, in1=part, op0=ALU.mult, op1=ALU.mult)
            last.then_inc(ctx_p, 1)
            for q in range(8):
                dve.wait_ge(ctx_num_mm, q + 1)
                finish_rows(bank[3], q, NL, q // 2, q % 2, ctx_num_out)
            masked(0)
            weighted(0)
            for q in range(8):
                if q + 1 < 8:
                    masked(q + 1)
                consume(q)
                if q + 1 < 8:
                    weighted(q + 1)
            dve.wait_ge(unit_out, 32)
            for n in range(20):
                last = V.bn_stats(bn[:, n, :], hsum[:, n // 4, (n % 4) * HD:(n % 4 + 1) * HD])
            then(last)
            for n in range(20):
                last = V.bn_aggr(mv[:, n, :], bn[:, n, :])
            then(last)
            V.tensor_scalar_add(rstd[:, :], mv[:, :, 1], EPS).then_inc(var_ready, 1)
            dve.wait_ge(std_ready, 1)
            then(V.reciprocal(rstd[:, :], rstd[:, :]))
            for n in range(20):
                v = hsum[:, n // 4, (n % 4) * HD:(n % 4 + 1) * HD]
                last = V.tensor_scalar(v, v, mv[:, n, 0:1], rstd[:, n:n + 1], ALU.subtract, ALU.mult)
            last.then_inc(hn_ready, 1)
            dve.wait_ge(sig_ready, 3)
            TB = ((6, 7), (4, 5))
            for k in range(KT):
                for (lo, hi), b, c in (((0, TL), 0, 1), ((TL, T), 1, 2)):
                    dve.wait_ge(hn_turned, 2 * k + c)
                    last = V.scalar_tensor_tensor(out=z[:, ZO + k, lo:hi], in0=bank[TB[k % 2][b]][:, 0:hi - lo], scalar=cols[:, 68 + k:69 + k],
                                                  in1=z[:, ZO + k, lo:hi], op0=ALU.mult, op1=ALU.mult)
                last.then_inc(yin_ready, 1)
            YB = ((0, 1, 2), (3, 4, 5))
            for m in range(KT):
                ba, bc, bb = YB[m % 2]
                dve.wait_ge(y_mm, m + 1)
                for base, latent, off in ((ZGA, ba, 0), (ZGB, bb, P)):
                    V.tensor_tensor(z[:, base + m, 0:TL], z[:, base + m, 0:TL], bank[latent][:, :], ALU.mult)
                    last = V.tensor_tensor(z[:, base + m, TL:T], z[:, base + m, TL:T], bank[bc][:, off:off + P], ALU.mult)
                last.then_inc(y_gated, 1)
            dve.wait_ge(rows1_loaded, 16 * 8)
            V.tensor_scalar_add(rows1[:, S2L:S2C + 1, :], rows1[:, S2L:S2C + 1, :], 1.0).then_inc(rows1_ready, 1)
            dve.wait_ge(xr_loaded, 32)

            def norm_in(tt, row, var_sem, std_sem, seen):
                for n in range(2):
                    last = V.bn_stats(bn[:, n, :], row[:, n * 512:(n + 1) * 512])
                then(last)
                then(V.bn_aggr(mv[:, tt, :], bn[:, 0:2, :]))
                V.tensor_scalar_add(rstd[:, tt:tt + 1], mv[:, tt, 1:2], EPS).then_inc(var_sem, 1)
                dve.wait_ge(std_sem, seen)
                then(V.reciprocal(rstd[:, tt:tt + 1], rstd[:, tt:tt + 1]))
                return V.tensor_scalar(row, row, mv[:, tt, 0:1], rstd[:, tt:tt + 1], ALU.subtract, ALU.mult)

            OB = ((6, 7), (0, 1))
            for tt in range(NT):
                c = 0 if tt < NL else 1
                for n in range(2):
                    dve.wait_ge(o_mm, 2 * tt + n + 1)
                    o = bank[OB[tt % 2][n]]
                    V.tensor_tensor(o[:, :], o[:, :], rows1[:, G1L + c, n * 512:(n + 1) * 512], ALU.mult).then_inc(dve_chain, 1)
                    chain[0] += 1
                dve.wait_ge(dve_chain, chain[0])
                for n in range(2):
                    o = bank[OB[tt % 2][n]]
                    row = xr[:, tt, n * 512:(n + 1) * 512]
                    last = V.scalar_tensor_tensor(out=row, in0=row, scalar=ALPHA, in1=o[:, :], op0=ALU.mult, op1=ALU.add)
                last.then_inc(o_out, 1)
                dve.wait_ge(o_out, tt + 1)
                norm_in(tt, xr[:, tt, :], ln_var, ln_std, tt + 1).then_inc(xn_ready, 1)
            dve.wait_ge(logits_mm, NT)
            dve.wait_ge(misc_loaded, 16 * 10)
            then(V.tensor_tensor(prob[:, :, :], bank[4][:, 0:NT * E].rearrange("p (t e) -> p t e", t=NT),
                                 br_bc[:, :].unsqueeze(1).to_broadcast([P, NT, E]), ALU.add))
            then(V.tensor_reduce(rs[:, 0, 0:NT], prob[:, :, :], AX, ALU.max))
            V.tensor_tensor(prob[:, :, :], prob[:, :, :], rs[:, 0, 0:NT].unsqueeze(2).to_broadcast([P, NT, E]), ALU.subtract).then_inc(soft_in, 1)
            dve.wait_ge(soft_out, 1)
            then(V.tensor_reduce(rs[:, 0, 0:NT], prob[:, :, :], AX, ALU.add))
            then(V.reciprocal(rs[:, 0, 0:NT], rs[:, 0, 0:NT]))
            then(V.tensor_tensor(prob[:, :, :], prob[:, :, :], rs[:, 0, 0:NT].unsqueeze(2).to_broadcast([P, NT, E]), ALU.mult))

            def wide(n):
                return rs[:, n, :].unsqueeze(2).to_broadcast([P, NT * EG, EPG])

            def groups(t):
                return t.rearrange("p t (g e) -> p (t g) e", g=EG)

            rev = rev4[:, :].unsqueeze(1).to_broadcast([P, NT * EG, EPG])
            pg = groups(prob[:, :, :])
            R = [groups(rt[:, n]) for n in range(6)]

            def first_max(values, top, mask, key):
                then(V.tensor_reduce(rs[:, top, :], values, AX, ALU.max))
                then(V.tensor_tensor(mask, values, wide(top), ALU.is_equal))
                then(V.tensor_tensor(mask, mask, rev, ALU.mult))
                then(V.tensor_reduce(rs[:, key, :], mask, AX, ALU.max))
                then(V.tensor_tensor(mask, mask, wide(key), ALU.is_equal))

            first_max(pg, 0, R[0], 1)
            then(V.scalar_tensor_tensor(out=R[1], in0=R[0], scalar=-2.0, in1=pg, op0=ALU.mult, op1=ALU.add))
            first_max(R[1], 2, R[2], 3)
            then(V.tensor_tensor(rs[:, 4, :], rs[:, 0, :], rs[:, 2, :], ALU.add))
            by_group = rs[:, 4, :].rearrange("p (t g) -> p t g", g=EG)
            mask_g = rs[:, 6, :].rearrange("p (t g) -> p t g", g=EG)
            rev_g = rev4[:, :].unsqueeze(1).to_broadcast([P, NT, EG])
            top_bc = rs[:, 5, 0:NT].unsqueeze(2).to_broadcast([P, NT, EG])
            then(V.tensor_reduce(rs[:, 5, 0:NT], by_group, AX, ALU.max))
            then(V.tensor_tensor(mask_g, by_group, top_bc, ALU.is_equal))
            then(V.tensor_tensor(mask_g, mask_g, rev_g, ALU.mult))
            then(V.tensor_reduce(rs[:, 5, 0:NT], mask_g, AX, ALU.max))
            then(V.tensor_tensor(mask_g, mask_g, top_bc, ALU.is_equal))
            then(V.reciprocal(rs[:, 7, :], rs[:, 4, :]))
            then(V.tensor_tensor(rs[:, 7, :], rs[:, 7, :], rs[:, 6, :], ALU.mult))
            for k, top in enumerate((0, 2)):
                then(V.tensor_tensor(rs[:, 8 + k, :], rs[:, top, :], rs[:, 7, :], ALU.mult))
                then(V.tensor_reduce(wtok[:, k, :], rs[:, 8 + k, :].rearrange("p (t g) -> p t g", g=EG), AX, ALU.add))
            then(V.tensor_tensor(R[0], R[0], wide(6), ALU.mult))
            then(V.tensor_tensor(R[2], R[2], wide(6), ALU.mult))
            V.tensor_tensor(R[5], R[0], R[2], ALU.add).then_inc(chosen, 1)
            dve.wait_ge(rank_mm, 1)
            cnt = bank[5][:, NT * E:(NT + 1) * E]
            then(V.tensor_tensor(cnt5[:, :, :], cnt.unsqueeze(2).to_broadcast([P, E, NT]), thresh[:, :].unsqueeze(1).to_broadcast([P, E, NT]), ALU.is_gt))
            then(V.tensor_reduce(est[:, 0, :], cnt5[:, :, :], AX, ALU.add))
            then(V.memset(est[:, 3, :], 0.0))
            then(V.tensor_tensor_scan(est[:, 1, :], est[:, 0, :], est[:, 3, :], 0.0, ALU.add, ALU.add))
            then(V.tensor_tensor(est[:, 2, :], est[:, 1, :], est[:, 0, :], ALU.subtract))
            then(V.tensor_scalar_mul(est[:, 2, :], est[:, 2, :], float(P)))
            then(V.tensor_tensor(rt[:, 3], bank[5][:, 0:NT * E].rearrange("p (t e) -> p t e", t=NT), est[:, 2, :].unsqueeze(1).to_broadcast([P, NT, E]), ALU.add))
            for k, n in enumerate((0, 2)):
                then(V.tensor_tensor(rt[:, 4], rt[:, 3], rt[:, n], ALU.mult))
                then(V.tensor_reduce(slot_f[:, k, :], rt[:, 4], AX, ALU.add))
            then(V.tensor_copy(slot_i[:, :], slot_f[:, :, :].rearrange("p k t -> p (k t)")))
            then(V.tensor_tensor(own[:, :, :], est[0:1, 1, :].unsqueeze(1).to_broadcast([1, SLOT_TILES, E]),
                                 tile_no[:, :].unsqueeze(2).to_broadcast([1, SLOT_TILES, E]), ALU.is_le))
            then(V.tensor_reduce(own_f[:, :], own[:, :, :], AX, ALU.add))
            then(V.tensor_scalar_min(own_f[:, :], own_f[:, :], float(E - 1)))
            then(V.tensor_copy(tile_expert[:, :], own_f[:, :]))
            then(V.tensor_copy(n_tiles[:, :], est[0:1, 1, E - 1:E]))
            V.tensor_scalar(half_tiles[:, :], n_tiles[:, :], 1, None, ALU.arith_shift_right).then_inc(slots_ready, 1)
            dve.wait_ge(table_loaded, 16)
            V.tensor_copy(slot_rows_f[:, :], slot_rows[:, :]).then_inc(table_f, 1)
            dve.wait_ge(table_turned, 1)
            V.tensor_copy(slot_tok[:, :], bank[7][:, 0:ROW_TILES]).then_inc(table_ready, 1)

            def rows_out(j, s):
                dve.wait_ge(hg_turned, j + 1)
                V.tensor_copy(hgT[s][:, 0:512], bank[2][:, :])
                V.tensor_copy(hgT[s][:, 512:D], bank[3][:, :]).then_inc(hgT_ready, 1)

            def product(j):
                dve.wait_ge(silu_ready, j + 1)
                dve.wait_ge(up_mm, j + 1)
                V.tensor_tensor(act_a, silu_g, bank[1][:, :], ALU.mult).then_inc(a_ready, 1)

            def aT_out(j):
                dve.wait_ge(a_turned, j + 1)
                V.tensor_copy(act_aT, bank[4][:, :]).then_inc(aT_ready, 1)

            def step(j, s):
                if not (isinstance(j, int) and j <= 1):
                    dve.wait_ge(down_mm, j - 1)
                aT_out(j - 1)
                product(j)
                rows_out(j + 1, 1 - s)

            half = half_run(dve)
            rows_out(0, 0)
            rows_out(1, 1)
            product(0)
            step(1, 1)
            step(2, 0)
            with dve.Fori(1, PAIRS) as i:
                with dve.If(i < half):
                    step(2 * i + 1, 1)
                    step(2 * i + 2, 0)
            dve.wait_ge(down_mm, 2 * half)
            aT_out(2 * half)
            dve.wait_ge(rows2_loaded, 64)
            for tt in range(NT):
                c = 0 if tt < NL else 1
                y0, y1 = yg[tt % 2]
                dve.wait_ge(yg_loaded[tt % 2], 32 * (tt // 2 + 1))
                then(V.tensor_scalar(y0, y0, wtok[:, 0, tt:tt + 1], None, ALU.mult))
                then(V.scalar_tensor_tensor(out=y0, in0=y1, scalar=wtok[:, 1, tt:tt + 1], in1=y0, op0=ALU.mult, op1=ALU.add))
                then(V.tensor_tensor(y0, y0, rows2[:, G2L + c, :], ALU.mult))
                then(V.scalar_tensor_tensor(out=y0, in0=xr[:, tt, :], scalar=ALPHA, in1=y0, op0=ALU.mult, op1=ALU.add))
                then(norm_in(tt, y0, fin_var, fin_std, tt + 1))
                then(V.tensor_tensor(y0, y0, rows2[:, LN2G, :], ALU.mult))
                V.tensor_tensor(y0, y0, rows2[:, LN2B, :], ALU.add).then_inc(out_ready, 1)


_INS = ["x_prompt", "x_sample", "state_C", "state_n", "state_m", "c", "c_ctx", "w_in", "b_in", "w_a", "w_b", "w_out",
        "g_head", "ln1_g", "ln1_b", "ln2_g", "ln2_b", "w_ada", "b_ada", "w_router", "b_router", "w_gate", "w_up", "w_down"]
_OUTS = [("y_prompt", (1, TC, D)), ("y_sample", (1, TL, D)), ("new_C", (1, 1, 2, H, HD, HD)), ("new_n", (1, 1, 2, H, HD)),
         ("new_m", (1, 1, 2, H))]


def kernel(**inputs):
    import concourse.bacc as _bacc
    from concourse.bass_utils import run_bass_kernel_spmd as _run

    nc = _bacc.Bacc("TRN2", target_bir_lowering=False, num_devices=1, dynamic_dma_scratch_size=8192)
    arrays = {n: np.ascontiguousarray(inputs[n]) for n in _INS}
    arrays["t128"], arrays["t512"] = dft_tables()
    args = {n: nc.dram_tensor(n, v.shape, F32, kind="ExternalInput").ap() for n, v in arrays.items()}
    for n, shape in _OUTS:
        args[n] = nc.dram_tensor(n, shape, F32, kind="ExternalOutput").ap()
    build(nc, args)
    r = _run(nc, [arrays], core_ids=[0])
    return tuple(r.results[0][n] for n, _ in _OUTS)
```

```python
from contextlib import ExitStack

import numpy as np

import concourse.bass as bass
from concourse import mybir

F32 = mybir.dt.float32
F32R = mybir.dt.float32r
I32 = mybir.dt.int32
ALU = mybir.AluOpType
ACT = mybir.ActivationFunctionType
AX = mybir.AxisListType.X

P = 128
D = 1024
KT = D // P
TL, TC = 512, 128
T = TL + TC
NT = T // P
NL = TL // P
H, HD = 4, 256
NZ = 52
ZQ, ZK, ZV, ZO, ZU, ZGA, ZGB = 0, 8, 16, 24, 32, 36, 44
GATE_OFF = NZ * P
NG, FD = 4, 128
E, EG, EPG = 16, 4, 4
DE = 512
SLOT_TILES = (2 * T + E * (P - 1)) // P
ROW_TILES = SLOT_TILES + 1
PAIRS = SLOT_TILES // 2
MIN_PAIRS = 2 * T // P // 2
ALPHA = 2.0 ** 0.25
EPS = 1e-6
NEG = -1.0e30
GR = 36
N_ADA = 6 * D // 512
ADA_SLOTS = 3
N_ZB = NZ // 4
TH = T // 2


def dft_tables():
    a = 2 * np.pi * ((np.arange(P)[:, None] * np.arange(P)[None]) % P) / P
    t128 = np.concatenate([np.cos(a), -np.sin(a), np.sin(a)], 1) / np.sqrt(P)
    b = 2 * np.pi * ((np.arange(TL)[:, None] * np.arange(TL)[None]) % TL) / TL
    t512 = np.stack([np.cos(b), np.sin(b)]) / np.sqrt(TL)
    return t128.astype(np.float32), t512.astype(np.float32)


def build(nc, a):
    ctx = ExitStack()
    with ctx:
        def sb(name, shape, dt=F32):
            return ctx.enter_context(nc.sbuf_tensor(name, shape, dt))

        def pb(name):
            return ctx.enter_context(nc.psum_tensor(name, [P, 512], F32))

        def sem(name):
            return ctx.enter_context(nc.semaphore(name))

        mod_d = nc.dram_tensor("mod_d", (2, 6 * D), F32, kind="Internal").ap()
        h2_d = nc.dram_tensor("h2_d", (T, D), F32, kind="Internal").ap()
        slot_tok_d = nc.dram_tensor("slot_tok_d", (ROW_TILES * P, 1), I32, kind="Internal").ap()
        y_d = nc.dram_tensor("y_d", (SLOT_TILES * P, D), F32, kind="Internal").ap()

        Z_AT = -(-nc.sbuf_base // 32) * 32
        R1_AT = Z_AT + 4 * NZ * T
        R2_AT = R1_AT + 4 * 5160
        R3_AT = R2_AT + 4 * 8192

        def at(name, shape, offset, dt=F32R):
            return nc.alloc_sbuf_tensor_at(name, shape, dt, offset=offset)

        z = sb("z", [P, NZ, T])
        r1 = sb("r1", [P, 5160])
        r2 = sb("r2", [P, 8192])
        r3 = sb("r3", [P, 5120])
        zf = z[:, :, :].rearrange("p f t -> p (f t)")

        hT_hi = at("hT_hi", [P, KT, T], R1_AT)
        hT_lo = at("hT_lo", [P, KT, T], R3_AT)
        w_hl = at("w_hl", [P, 2, 2, KT, P], R2_AT)
        raw = [r2[:, 4096 + s * 2048:4096 + (s + 1) * 2048].rearrange("p (k n) -> p k n", k=KT) for s in range(2)]
        stack = zf[0:92, 0:P]
        wgate_raw = zf[:, 128:256].rearrange("p (k n) -> p k n", k=KT)
        wgate = zf[:, 256:1280].rearrange("p (k n) -> p k n", k=KT)
        zero_i = zf[0:ROW_TILES, 1280:1408].bitcast(I32)
        x_sb = zf[:, 2048:7168].rearrange("p (t d) -> p t d", t=NT)
        h_tmp = [zf[:, 7168 + s * T:7168 + (s + 1) * T] for s in range(2)]
        wgate_hl = at("wgate_hl", [P, 2, KT, P], Z_AT + 4 * 8448)
        ada_ring = [w.rearrange("p (k n) -> p k n", k=KT) for w in (zf[:, 10496:14592], zf[:, 14592:18688], r2[:, 0:4096])]
        mod = zf[0:2, 33280 - 12288:33280 - 6144]
        b_ada = zf[0:2, 33280 - 6144:33280]
        gate_i, gate_f, log_f, tmp_g, b_row, m_row, zero_row, bm_row = (zf[0:GR, 28160 + n * T:28160 + (n + 1) * T] for n in range(8))
        vaug = r1[:, 0:NT * H * 257].rearrange("p (t h v) -> p t h v", t=NT, h=H)
        c0_raw = r2[:, 0:4096].rearrange("p (j b k) -> p j b k", j=8, b=2)
        c0T = zf[:, ZV * T:ZV * T + 8 * 2 * 257].rearrange("p (j b v) -> p j b v", j=8, b=2)
        dp = [r2[:, s * 2048:(s + 1) * 2048].rearrange("p (s t) -> p s t", s=NL) for s in range(2)]
        qs = [r2[:, 4096 + s * 1024:4096 + (s + 1) * 1024].rearrange("p (b t) -> p b t", b=2) for s in range(2)]
        md = r2[:, 6144:6656]
        wq = r2[:, 6656:7168]
        ktok = r2[:, 7168:8192]
        dc = r2[:, 0:1024].rearrange("p (j t) -> p j t", j=8)
        mdc = r2[:, 2048:3072].rearrange("p (j t) -> p j t", j=8)
        c_out = [r2[:, 3072 + s * HD:3072 + (s + 1) * HD] for s in range(2)]
        n_out = [r2[0:1, 3584 + s * HD:3584 + (s + 1) * HD] for s in range(2)]
        wv = r2[:, 4096:6144].rearrange("p (j v) -> p j v", j=8)
        hsum = r3[:, :].rearrange("p (t d) -> p t d", t=NT)
        four_a = zf[:, 0:NT * NG * 256].rearrange("p (t g c f) -> p t g c f", t=NT, g=NG, c=2)
        four_l = zf[:, ZK * T:ZK * T + 4096].rearrange("p (c s t) -> p c s t", c=2, s=NL)
        t128_sb = zf[:, ZK * T + 4096:ZK * T + 4096 + 3 * P]
        wa_sb = r2[:, :].rearrange("p (k n) -> p k n", k=KT)
        wb_sb = r1[:, 0:4096].rearrange("p (k n) -> p k n", k=4)
        wo_sb = zf[:, 0:8192].rearrange("p (k n) -> p k n", k=KT)
        xr = r3[:, :].rearrange("p (t d) -> p t d", t=NT)
        rows1 = r2[:, :].rearrange("p (r d) -> p r d", r=8)
        G1L, G1C, S2L, S2C, H2L, H2C, LN1G, LN1B = range(8)
        h2 = r1[:, 0:5120].rearrange("p (t d) -> p t d", t=NT)
        h2T = [zf[:, 8192 + s * 1024:8192 + (s + 1) * 1024].rearrange("p (k t) -> p k t", k=KT) for s in range(2)]
        prob = r2[:, 0:80].rearrange("p (t e) -> p t e", t=NT)
        rt = r2[:, 80:560].rearrange("p (n t e) -> p n t e", n=6, t=NT)
        rs = r2[:, 560:800].rearrange("p (n g) -> p n g", n=12)
        cnt5 = r2[:, 800:880].rearrange("p (e t) -> p e t", e=E)
        est = r2[:, 880:944].rearrange("p (n e) -> p n e", n=4)
        own = r2[0:1, 944:944 + ROW_TILES * E].rearrange("p (j e) -> p j e", e=E)
        slot_rows = r2[0:ROW_TILES, 6144:6272].bitcast(I32)
        slot_rows_f = r2[0:ROW_TILES, 6272:6400]
        g_hl = at("g_hl", [P, 2, KT, DE], Z_AT)
        u_hl = at("u_hl", [P, 2, KT, DE], Z_AT + 32768)
        d_hl = at("d_hl", [P, 2, 4, D], Z_AT + 65536)
        g_raw, u_raw, d_raw = zf[:, 24576:28672], zf[:, 28672:32768], r2[:, 0:4096]
        silu_g = zf[:, 32768:33280]
        hg = [r2[:, 4096 + s * 1024:5120 + s * 1024] for s in range(2)]
        hgT_hl = at("hgT_hl", [P, 2, D], R2_AT + 4 * 6144)
        y_sb = [r1[:, s * 1024:(s + 1) * 1024] for s in range(2)]
        act_a = r1[:, 2048:2560]
        aT_hl = at("aT_hl", [P, 2, DE], R1_AT + 4 * 2560)
        rows2 = zf[:, 0:4096].rearrange("p (r d) -> p r d", r=4)
        G2L, G2C, LN2G, LN2B = range(4)
        yg = [[r2[:, (s * 2 + k) * 1024:(s * 2 + k + 1) * 1024] for k in range(2)] for s in range(2)]

        ident = sb("ident", [P, P])
        mask_neg = sb("mask_neg", [P, 2, P])
        before = sb("before", [P, P])
        ones = sb("ones", [P, P])
        zeros = sb("zeros", [P, P])
        cols = sb("cols", [P, 92])
        cond = sb("cond", [P, 16])
        mcols = sb("mcols", [P, 16, 2])
        gbias = sb("gbias", [GR, 2])
        m0_col = sb("m0_col", [GR, 1])
        m0_bc = sb("m0_bc", [P, 8])
        neg_m = sb("neg_m", [GR, T])
        a_col = sb("a_col", [P, NT, GR])
        em_col = sb("em_col", [P, NT, GR])
        w_col = sb("w_col", [P, 8])
        den = sb("den", [P, 4])
        bn = sb("bn", [P, 20, 6])
        mv = sb("mv", [P, 20, 2])
        rstd = sb("rstd", [P, 20])
        wr_sb = sb("wr_sb", [P, KT, E])
        br_bc = sb("br_bc", [P, E])
        rev4 = sb("rev4", [P, EPG])
        thresh = sb("thresh", [P, NT])
        tile_no = sb("tile_no", [1, ROW_TILES])
        own_f = sb("own_f", [1, ROW_TILES])
        tile_expert = sb("tile_expert", [1, ROW_TILES], I32)
        slot_f = sb("slot_f", [P, 2, NT])
        slot_i = sb("slot_i", [P, 2 * NT], I32)
        wtok = sb("wtok", [P, 2, NT])
        tok_id = sb("tok_id", [P, NT], I32)
        slot_tok = sb("slot_tok", [P, ROW_TILES], I32)
        n_tiles = sb("n_tiles", [1, 1], I32)
        half_tiles = sb("half_tiles", [1, 1], I32)
        tok_cell = [sb(f"tok_cell{s}", [P, 1], I32) for s in range(2)]

        bank = [pb(f"bank{n}") for n in range(8)]

        pool_setup = sem("pool_setup")
        stack_loaded = sem("stack_loaded")
        x_loaded = sem("x_loaded")
        bada_loaded = sem("bada_loaded")
        misc_loaded = sem("misc_loaded")
        raw_full = [sem(f"raw_full{s}") for s in range(2)]
        w_hi = sem("w_hi")
        w_lo = sem("w_lo")
        w_used = sem("w_used")
        ada_full = [sem(f"ada_full{s}") for s in range(ADA_SLOTS)]
        ada_mm = sem("ada_mm")
        wgate_hi = sem("wgate_hi")
        wgate_lo = sem("wgate_lo")
        h_full = sem("h_full")
        h_hi = sem("h_hi")
        stack_turned = sem("stack_turned")
        cols_ready = sem("cols_ready")
        cond_ready = sem("cond_ready")
        mod_ready = sem("mod_ready")
        mod_stored = sem("mod_stored")
        mod_turned = sem("mod_turned")
        mcols_ready = sem("mcols_ready")
        x_turned = sem("x_turned")
        hT_ready = sem("hT_ready")
        wgate_ready = sem("wgate_ready")
        gates_mm = sem("gates_mm")
        gates_out = sem("gates_out")
        z_mm = sem("z_mm")
        z_out = sem("z_out")
        z_out2 = sem("z_out2")
        act_chain = sem("act_chain")
        dve_chain = sem("dve_chain")
        pool_chain = sem("pool_chain")
        gate_exp = sem("gate_exp")
        gate_abs = sem("gate_abs")
        gate_rows = sem("gate_rows")
        gate_turned = sem("gate_turned")
        gate_cols = sem("gate_cols")
        v_turned = sem("v_turned")
        v_out = sem("v_out")
        v_out_dve = sem("v_out_dve")
        k_turned = sem("k_turned")
        k_out = sem("k_out")
        c0_loaded = sem("c0_loaded")
        c0_turned = sem("c0_turned")
        c0_out = sem("c0_out")
        n0_out = sem("n0_out")
        s_mm = sem("s_mm")
        m_mm = sem("m_mm")
        md_ready = sem("md_ready")
        d_ready = sem("d_ready")
        p_ready = sem("p_ready")
        unit_mm = sem("unit_mm")
        unit_out = sem("unit_out")
        ctx_mm = sem("ctx_mm")
        ctx_md = sem("ctx_md")
        ctx_d = sem("ctx_d")
        ctx_p = sem("ctx_p")
        ctx_num_mm = sem("ctx_num_mm")
        ctx_num_out = sem("ctx_num_out")
        state_mm = sem("state_mm")
        state_out = sem("state_out")
        state_stored = [sem(f"state_stored{s}") for s in range(2)]
        n_stored = [sem(f"n_stored{s}") for s in range(2)]
        small_stored = sem("small_stored")
        four_loaded = sem("four_loaded")
        four_a_mm = sem("four_a_mm")
        four_a_out = sem("four_a_out")
        four_mm = sem("four_mm")
        four_out = sem("four_out")
        sig_ready = sem("sig_ready")
        var_ready = sem("var_ready")
        std_ready = sem("std_ready")
        hn_ready = sem("hn_ready")
        hn_turned = sem("hn_turned")
        yin_ready = sem("yin_ready")
        wab_loaded = sem("wab_loaded")
        wo_loaded = sem("wo_loaded")
        y_mm = sem("y_mm")
        y_gated = sem("y_gated")
        merged = sem("merged")
        xr_loaded = sem("xr_loaded")
        rows1_loaded = sem("rows1_loaded")
        rows1_ready = sem("rows1_ready")
        o_mm = sem("o_mm")
        o_out = sem("o_out")
        ln_var = sem("ln_var")
        ln_std = sem("ln_std")
        xn_ready = sem("xn_ready")
        x1_ready = sem("x1_ready")
        h2_ready = sem("h2_ready")
        h2_stored = sem("h2_stored")
        h2_turned = sem("h2_turned")
        h2T_ready = sem("h2T_ready")
        logits_mm = sem("logits_mm")
        soft_in = sem("soft_in")
        soft_out = sem("soft_out")
        chosen = sem("chosen")
        rank_mm = sem("rank_mm")
        slots_ready = sem("slots_ready")
        zeros_stored = sem("zeros_stored")
        table_stored = sem("table_stored")
        table_loaded = sem("table_loaded")
        table_f = sem("table_f")
        table_turned = sem("table_turned")
        table_ready = sem("table_ready")
        wg_full, wu_full, wd_full = sem("wg_full"), sem("wu_full"), sem("wd_full")
        g_hi, u_hi, d_hi = sem("g_hi"), sem("u_hi"), sem("d_hi")
        g_lo, u_lo, d_lo = sem("g_lo"), sem("u_lo"), sem("d_lo")
        rows_hi, aT_hi = sem("rows_hi"), sem("aT_hi")
        hg_full = [sem(f"hg_full{s}") for s in range(2)]
        cell_ready = sem("cell_ready")
        cell_seen = sem("cell_seen")
        hg_turned = sem("hg_turned")
        hgT_ready = sem("hgT_ready")
        gate_mm = sem("gate_mm")
        up_mm = sem("up_mm")
        silu_ready = sem("silu_ready")
        a_ready = sem("a_ready")
        a_turned = sem("a_turned")
        aT_ready = sem("aT_ready")
        down_mm = sem("down_mm")
        y_out = sem("y_out")
        zeros_ready = sem("zeros_ready")
        y_zeroed = sem("y_zeroed")
        y_stored = [sem(f"y_stored{s}") for s in range(2)]
        rows2_loaded = sem("rows2_loaded")
        yg_loaded = [sem(f"yg_loaded{s}") for s in range(2)]
        yg_free = sem("yg_free")
        fin_var = sem("fin_var")
        fin_std = sem("fin_std")
        out_ready = sem("out_ready")
        out_stored = [sem(f"out_stored{s}") for s in range(2)]

        def half_run(eng):
            eng.wait_ge(slots_ready, 1)
            return eng.value_load(half_tiles[0:1, 0:1], min_val=MIN_PAIRS, max_val=PAIRS)

        def gate_row(j):
            return j if j < 4 else 28 + j

        block = ctx.enter_context(nc.Block())

        @block.sync
        def _(sp):
            sp.dma_start(stack[0:8, :], a["c"].rearrange("b (k p) -> (b k) p", p=P)).then_inc(stack_loaded, 16)
            sp.dma_start(stack[8:16, :], a["c_ctx"].rearrange("(k p) -> k p", p=P)).then_inc(stack_loaded, 16)
            sp.dma_start(stack[16:68, :], a["b_in"][0, 0:GATE_OFF].rearrange("(k p) -> k p", p=P)).then_inc(stack_loaded, 16)
            sp.dma_start(stack[68:76, :], a["g_head"][0, :].rearrange("(k p) -> k p", p=P)).then_inc(stack_loaded, 16)
            sp.dma_start(stack[76:92, :], a["state_n"].rearrange("a b d h (k p) -> (a b d h k) p", p=P)).then_inc(stack_loaded, 16)

            def load_raw(src, col, s):
                sp.dma_start(raw[s], src[0, :, bass.ds(col, 256)].rearrange("(k p) n -> p k n", p=P)).then_inc(raw_full[s], 16)

            def load_ada(n, s):
                sp.dma_start(ada_ring[s], a["w_ada"][0, :, bass.ds(512 * n, 512)].rearrange("(k p) n -> p k n", p=P)).then_inc(ada_full[s], 16)

            for s in range(ADA_SLOTS):
                load_ada(s, s)
            sp.dma_start(b_ada, a["b_ada"][0, :].partition_broadcast(2)).then_inc(bada_loaded, 16)
            sp.dma_start(x_sb[:, 0:NL, :], a["x_sample"][0].rearrange("(t p) d -> p t d", p=P)).then_inc(x_loaded, 16)
            sp.dma_start(x_sb[:, NL, :], a["x_prompt"][0]).then_inc(x_loaded, 16)
            with sp.Fori(1, N_ADA // ADA_SLOTS) as i:
                for s in range(ADA_SLOTS):
                    sp.wait_ge(ada_mm, ADA_SLOTS * i + s - (ADA_SLOTS - 1))
                    load_ada(ADA_SLOTS * i + s, s)
            for s in range(2):
                load_raw(a["w_in"], 256 * s, s)
            with sp.Fori(1, N_ZB) as i:
                for s in range(2):
                    sp.wait_ge(w_lo, 4 * i + 2 * s - 2)
                    load_raw(a["w_in"], 512 * i + 256 * s, s)
            sp.wait_ge(zeros_ready, 1)
            always = 2 * MIN_PAIRS + 1
            sp.dma_start(y_d[always * P:, :].rearrange("(p r) (c n) -> p (r c) n", p=P, n=P),
                         zeros[:, :].unsqueeze(1).to_broadcast([P, (SLOT_TILES - always) * KT, P])).then_inc(y_zeroed, 16)
            sp.wait_ge(w_used, NZ)
            sp.dma_start(c0_raw, a["state_C"].rearrange("a b d h (v p) k -> p (a b d h) v k", p=P)).then_inc(c0_loaded, 16)
            sp.wait_ge(s_mm, H)
            sp.wait_ge(k_turned, 2)
            sp.dma_start(four_l, a["t512"].rearrange("c (s p) t -> p c s t", p=P)).then_inc(four_loaded, 16)
            sp.dma_start(t128_sb, a["t128"]).then_inc(four_loaded, 16)
            sp.wait_ge(unit_mm, 32)
            sp.dma_start(wb_sb, a["w_b"][0].rearrange("(k p) n -> p k n", p=P)).then_inc(wab_loaded, 16)
            sp.dma_start(wa_sb, a["w_a"][0].rearrange("(k p) n -> p k n", p=P)).then_inc(wab_loaded, 16)
            sp.wait_ge(four_mm, NG)
            sp.dma_start(wo_sb, a["w_out"][0].rearrange("(k p) n -> p k n", p=P)).then_inc(wo_loaded, 16)
            sp.wait_ge(hn_turned, 2 * KT)
            sp.dma_start(xr[:, 0:NL, :], a["x_sample"][0].rearrange("(t p) d -> p t d", p=P)).then_inc(xr_loaded, 16)
            sp.dma_start(xr[:, NL, :], a["x_prompt"][0]).then_inc(xr_loaded, 16)
            sp.wait_ge(y_mm, KT)
            sp.wait_ge(mod_stored, 16)
            for r, src in ((G1L, mod_d[0, 2 * D:3 * D]), (G1C, mod_d[1, 2 * D:3 * D]), (S2L, mod_d[0, 4 * D:5 * D]),
                           (S2C, mod_d[1, 4 * D:5 * D]), (H2L, mod_d[0, 3 * D:4 * D]), (H2C, mod_d[1, 3 * D:4 * D]),
                           (LN1G, a["ln1_g"][0, :]), (LN1B, a["ln1_b"][0, :])):
                sp.dma_start(rows1[:, r, :], src.partition_broadcast(P)).then_inc(rows1_loaded, 16)
            for tt in range(NT):
                sp.wait_ge(h2_ready, tt + 1)
                sp.dma_start(h2_d[tt * P:(tt + 1) * P, :], h2[:, tt, :]).then_inc(h2_stored, 16)
            sp.wait_ge(table_stored, 16 * 2 * NT)
            sp.dma_start(slot_rows[:, :], slot_tok_d.rearrange("(j p) o -> j (p o)", p=P)).then_inc(table_loaded, 16)
            sp.wait_ge(slots_ready, 1)
            sp.wait_ge(h2T_ready, 2 * NT)
            sp.wait_ge(logits_mm, NT)

            half = half_run(sp)

            def expert_of(j):
                return sp.value_load(tile_expert[0:1, bass.ds(j, 1)], min_val=0, max_val=E - 1)

            def load_gate_up(j):
                e = expert_of(j)
                for w, name, full, lo in ((g_raw, "w_gate", wg_full, g_lo), (u_raw, "w_up", wu_full, u_lo)):
                    if not (isinstance(j, int) and j == 0):
                        sp.wait_ge(lo, 2 * j)
                    sp.dma_start(w.rearrange("p (k n) -> p k n", k=KT), a[name][0][bass.ds(e, 1)].rearrange("e (k p) n -> p (e k) n", p=P)).then_inc(full, 16)

            def load_down(j):
                e = expert_of(j)
                if not (isinstance(j, int) and j == 0):
                    sp.wait_ge(d_lo, 2 * j)
                sp.dma_start(d_raw.rearrange("p (k n) -> p k n", k=4), a["w_down"][0][bass.ds(e, 1)].rearrange("e (k p) n -> p (e k) n", p=P)).then_inc(wd_full, 16)

            load_gate_up(0)
            for j in range(3):
                load_gate_up(j + 1)
                load_down(j)
            with sp.Fori(1, PAIRS) as i:
                with sp.If(i < half):
                    for s in (1, 2):
                        load_gate_up(2 * i + s + 1)
                        load_down(2 * i + s)
            sp.wait_ge(up_mm, 2 * half + 1)
            sp.wait_ge(g_lo, 4 * half + 4)
            sp.wait_ge(u_lo, 4 * half + 4)
            for r, src in ((G2L, mod_d[0, 5 * D:6 * D]), (G2C, mod_d[1, 5 * D:6 * D]),
                           (LN2G, a["ln2_g"][0, :]), (LN2B, a["ln2_b"][0, :])):
                sp.dma_start(rows2[:, r, :], src.partition_broadcast(P)).then_inc(rows2_loaded, 16)
            for tt in range(NT):
                sp.wait_ge(out_ready, tt + 1)
                dst = a["y_sample"][0, tt * P:(tt + 1) * P, :] if tt < NL else a["y_prompt"][0]
                sp.dma_start(dst, yg[tt % 2][0]).then_inc(out_stored[tt % 2], 16)
            sp.wait_ge(out_stored[0], 16 * 3)
            sp.wait_ge(out_stored[1], 16 * 2)
            sp.wait_ge(small_stored, 32)
            for s in range(2):
                sp.wait_ge(n_stored[s], 4 * 16)
                sp.wait_ge(state_stored[s], 8 * 16)

        @block.gpsimd
        def _(pool):
            chain = [0]

            def then(ins):
                chain[0] += 1
                ins.then_inc(pool_chain, 1)
                pool.wait_ge(pool_chain, chain[0])

            nc.gpsimd.dma_start(wgate_raw[:, :, :], a["w_in"][0, :, GATE_OFF:GATE_OFF + 16].rearrange("(k p) n -> p k n", p=P)).then_inc(misc_loaded, 16)
            then(nc.gpsimd.memset(gbias[:, :], 0.0))
            with nc.allow_non_contiguous_dma(reason="a few words"):
                for kind in range(2):
                    for d in range(2):
                        c = GATE_OFF + 8 * kind + 4 * d
                        nc.gpsimd.dma_start(gbias[32 * d:32 * d + 4, kind:kind + 1], a["b_in"][0, c:c + 4].rearrange("(h o) -> h o", o=1)).then_inc(misc_loaded, 16)
                for d in range(2):
                    nc.gpsimd.dma_start(m0_col[32 * d:32 * d + 4, :], a["state_m"][0, 0, d, :].rearrange("(h o) -> h o", o=1)).then_inc(misc_loaded, 16)
            nc.gpsimd.dma_start(m0_bc[:, :], a["state_m"].rearrange("a b d h -> (a b d h)").partition_broadcast(P)).then_inc(misc_loaded, 16)
            nc.gpsimd.dma_start(wr_sb[:, :, :], a["w_router"].rearrange("(k p) n -> p k n", p=P)).then_inc(misc_loaded, 16)
            nc.gpsimd.dma_start(br_bc[:, :], a["b_router"].partition_broadcast(P)).then_inc(misc_loaded, 16)
            then(nc.gpsimd.memset(ident[:, :], 0.0))
            nc.gpsimd.affine_select(out=ident[:, :], in_=ident[:, :], compare_op=ALU.not_equal, fill=1.0, base=0,
                                    pattern=[[-1, P]], channel_multiplier=1).then_inc(pool_setup, 1)
            nc.gpsimd.memset(ones[:, :], 1.0).then_inc(pool_setup, 1)
            nc.gpsimd.memset(zeros[:, :], 0.0).then_inc(zeros_ready, 1)
            then(nc.gpsimd.memset(mask_neg[:, :, :], 0.0))
            for d in range(2):
                m = mask_neg[:, d, :]
                sign = 1 if d == 0 else -1
                nc.gpsimd.affine_select(out=m, in_=m, compare_op=ALU.is_ge, fill=NEG, base=0,
                                        pattern=[[sign, P]], channel_multiplier=-sign).then_inc(pool_setup, 1)
            then(nc.gpsimd.memset(before[:, :], 1.0))
            nc.gpsimd.affine_select(out=before[:, :], in_=before[:, :], compare_op=ALU.is_gt, fill=0.0, base=0,
                                    pattern=[[1, P]], channel_multiplier=-1).then_inc(pool_setup, 1)
            nc.gpsimd.iota(tok_id[:, :], pattern=[[P, NT]], base=0, channel_multiplier=1).then_inc(pool_setup, 1)
            nc.gpsimd.memset(zero_i[:, :], 0).then_inc(pool_setup, 1)
            for i in range(EPG):
                then(nc.gpsimd.memset(rev4[:, i:i + 1], float(EPG - i)))
            for i in range(NT):
                then(nc.gpsimd.memset(thresh[:, i:i + 1], float(P * i)))
            nc.gpsimd.iota(tile_expert[:, :], pattern=[[1, ROW_TILES]], base=0, channel_multiplier=0).then_inc(pool_setup, 1)
            pool.wait_ge(pool_setup, 8)
            nc.gpsimd.tensor_copy(tile_no[:, :], tile_expert[:, :]).then_inc(pool_setup, 1)
            nc.gpsimd.dma_start(slot_tok_d.rearrange("(j p) o -> j (p o)", p=P), zero_i[:, :]).then_inc(zeros_stored, 16)
            pool.wait_ge(pool_setup, 9)
            nc.gpsimd.memset(wgate[:, :, :], 0.0).then_inc(pool_setup, 1)
            pool.wait_ge(mod_ready, N_ADA)
            nc.gpsimd.dma_start(mod_d, mod).then_inc(mod_stored, 16)
            pool.wait_ge(gate_rows, 1)
            with nc.allow_non_contiguous_dma(reason="a few words"):
                nc.gpsimd.dma_start(a["new_m"][0, 0, 0, :].rearrange("(h o) -> h o", o=1), bm_row[0:4, T - 1:T]).then_inc(small_stored, 16)
                nc.gpsimd.dma_start(a["new_m"][0, 0, 1, :].rearrange("(h o) -> h o", o=1), bm_row[32:36, TL:TL + 1]).then_inc(small_stored, 16)
            for q in range(8):
                h, d = q // 2, q % 2
                for vb in range(2):
                    pool.wait_ge(state_out, 3 * q + vb + 1)
                    nc.gpsimd.dma_start(a["new_C"][0, 0, d, h, vb * P:(vb + 1) * P, :], c_out[vb]).then_inc(state_stored[vb], 16)
                pool.wait_ge(state_out, 3 * q + 3)
                nc.gpsimd.dma_start(a["new_n"][0, 0, d, h:h + 1, :], n_out[q % 2]).then_inc(n_stored[q % 2], 16)
            for m in range(KT):
                pool.wait_ge(y_gated, m + 1)
                nc.gpsimd.tensor_tensor(z[:, ZGA + m, :], z[:, ZGA + m, :], z[:, ZGB + m, :], ALU.add).then_inc(merged, 1)
            pool.wait_ge(rows1_ready, 1)
            for tt in range(NT):
                c = 0 if tt < NL else 1
                pool.wait_ge(xn_ready, tt + 1)
                then(nc.gpsimd.tensor_tensor(xr[:, tt, :], xr[:, tt, :], rows1[:, LN1G, :], ALU.mult))
                then(nc.gpsimd.tensor_tensor(xr[:, tt, :], xr[:, tt, :], rows1[:, LN1B, :], ALU.add))
                then(nc.gpsimd.tensor_tensor(h2[:, tt, :], xr[:, tt, :], rows1[:, S2L + c, :], ALU.mult))
                nc.gpsimd.tensor_tensor(h2[:, tt, :], h2[:, tt, :], rows1[:, H2L + c, :], ALU.add).then_inc(h2_ready, 1)
            pool.wait_ge(zeros_stored, 16)
            pool.wait_ge(slots_ready, 1)
            for n in range(2 * NT):
                nc.gpsimd.indirect_dma_start(slot_tok_d, bass.IndirectOffsetOnAxis(ap=slot_i[:, n:n + 1], axis=0),
                                             tok_id[:, n % NT:n % NT + 1], None).then_inc(table_stored, 16)
            pool.wait_ge(table_ready, 1)
            pool.wait_ge(h2_stored, 16 * NT)
            pool.wait_ge(logits_mm, NT)
            pool.wait_ge(merged, KT)
            pool.wait_ge(o_mm, 2 * NT)

            def gather(j, s):
                nc.gpsimd.tensor_copy(tok_cell[s][:, :], slot_tok[:, bass.ds(j, 1)]).then_inc(cell_ready, 1)
                pool.wait_ge(cell_ready, j + 1)
                pool.sem_inc(cell_seen, 1)
                nc.gpsimd.indirect_dma_start(hg[s], None, h2_d, bass.IndirectOffsetOnAxis(ap=tok_cell[s][:, :], axis=0)).then_inc(hg_full[s], 16)

            half = half_run(pool)
            gather(0, 0)
            gather(1, 1)
            with pool.Fori(1, PAIRS + 1) as i:
                with pool.If(i < half + 1):
                    for s in range(2):
                        pool.wait_ge(hg_full[s], 16 * i)
                        pool.wait_ge(hg_turned, 2 * i + s - 1)
                        gather(2 * i + s, s)
            pool.wait_ge(y_stored[0], 16 * half + 16)
            pool.wait_ge(y_stored[1], 16 * half)
            pool.sem_inc(cell_seen, 1)
            for tt in range(NT):
                if tt >= 2:
                    pool.wait_ge(out_stored[tt % 2], 16 * (tt // 2))
                for k in range(2):
                    nc.gpsimd.indirect_dma_start(yg[tt % 2][k], None, y_d, bass.IndirectOffsetOnAxis(ap=slot_i[:, k * NT + tt:k * NT + tt + 1], axis=0)).then_inc(yg_loaded[tt % 2], 16)

        @block.scalar
        def _(act):
            A = nc.scalar.activation
            chain = [0]

            def then(ins):
                chain[0] += 1
                ins.then_inc(act_chain, 1)
                act.wait_ge(act_chain, chain[0])

            act.wait_ge(cols_ready, 1)
            A(cond[:, :], cols[:, 0:16], ACT.Silu).then_inc(cond_ready, 1)

            def high(full, f, first=False, u=None):
                if f % 2 == 0:
                    act.wait_ge(raw_full[f // 2], 16 * full)
                if not first:
                    act.wait_ge(w_used, u - 1)
                A(w_hl[:, f % 2, 0], raw[f // 2][:, :, (f % 2) * P:(f % 2 + 1) * P], ACT.Copy).then_inc(w_hi, 1)

            act.wait_ge(wgate_ready, 1)
            A(wgate_hl[:, 0], wgate, ACT.Copy).then_inc(wgate_hi, 1)
            act.wait_ge(mcols_ready, 1)
            for k in range(KT):
                act.wait_ge(x_turned, k + 1)
                if k >= 2:
                    act.wait_ge(hT_ready, k - 1)
                A(h_tmp[k % 2][:, 0:TL], bank[2 + k % 2][:, :], ACT.Identity, scale=mcols[:, 8 + k, 0:1], bias=mcols[:, k, 0:1])
                A(h_tmp[k % 2][:, TL:T], bank[4 + k % 2][:, 0:P], ACT.Identity, scale=mcols[:, 8 + k, 1:2], bias=mcols[:, k, 1:2]).then_inc(h_full, 1)
                act.wait_ge(h_full, k + 1)
                A(hT_hi[:, k, :], h_tmp[k % 2], ACT.Copy).then_inc(h_hi, 1)
            act.wait_ge(ada_mm, N_ADA)
            for f in range(2):
                high(1, f, first=True)
            act.wait_ge(mod_stored, 16)
            act.wait_ge(zeros_stored, 16)
            act.wait_ge(gates_mm, 1)
            for n, dst in enumerate((gate_i, gate_f)):
                for b in range(2):
                    A(dst[:, b * TH:(b + 1) * TH], bank[6 + b][64 * n:64 * n + GR, 0:TH], ACT.Copy).then_inc(gates_out, 1)
            act.wait_ge(gate_abs, 1)
            then(A(tmp_g, tmp_g, ACT.Exp))
            A(tmp_g, tmp_g, ACT.Ln, bias=ones[0:GR, 0:1]).then_inc(gate_exp, 1)

            def z_block(b, last=False):
                for f in range(4):
                    act.wait_ge(z_mm, 4 * b + f + 1)
                    A(z[:, bass.ds(4 * b + f, 1), 0:TH].rearrange("p a t -> p (a t)"), bank[2 * f][:, 0:TH], ACT.Identity,
                      bias=cols[:, bass.ds(16 + 4 * b + f, 1)]).then_inc(z_out, 1)
                    if not last or f < 2:
                        high(b + 1 + (f + 2) // 4, (f + 2) % 4, u=4 * b + f + 2)

            for b in range(2):
                z_block(b)
            act.wait_ge(gate_turned, 1)
            A(em_col[:, :, :], bank[7][:, 0:5 * GR].rearrange("p (t g) -> p t g", t=NT), ACT.Exp, scale=-1.0).then_inc(gate_cols, 1)
            with act.Fori(2, N_ZB - 2) as i:
                z_block(i)
            act.wait_ge(small_stored, 32)
            z_block(N_ZB - 2)
            z_block(N_ZB - 1, last=True)
            for n in range(10):
                if n % 2 == 0:
                    act.wait_ge(v_turned, n + 1)
                    A(vaug[:, n // 2, 0:2, 0:HD], bank[n % 4][:, :].rearrange("p (h v) -> p h v", h=2), ACT.Copy).then_inc(v_out, 1)
            for n in range(2):
                act.wait_ge(k_turned, n + 1)
                A(ktok[:, n * 512:(n + 1) * 512], bank[4 + n][:, :], ACT.Copy, scale=HD ** -0.5).then_inc(k_out, 1)
            for j in range(8):
                act.wait_ge(c0_turned, j + 1)
                A(c0T[:, j, :, 0:HD], bank[j % 4][:, :].rearrange("p (b v) -> p b v", b=2), ACT.Copy).then_inc(c0_out, 1)

            def decay(q):
                h, d = q // 2, q % 2
                j = d * 4 + h
                r = gate_row(j)
                act.wait_ge(md_ready, q + 1)
                if q == 1:
                    for s in range(2):
                        act.wait_ge(state_stored[s], 8 * 16)
                        act.wait_ge(n_stored[s], 4 * 16)
                if q >= 2:
                    act.wait_ge(unit_mm, 4 * (q - 1))
                for s in range(NL):
                    A(dp[q % 2][:, s, s * P:(s + 1) * P], md[:, s * P:(s + 1) * P], ACT.Exp, bias=a_col[:, s, r:r + 1])
                    lo, hi = ((s + 1) * P, TL) if d == 0 else (0, s * P)
                    if hi > lo:
                        A(dp[q % 2][:, s, lo:hi], bank[4][:, lo:hi], ACT.Exp, bias=a_col[:, s, r:r + 1])
                if q >= 1:
                    act.wait_ge(p_ready, q)
                A(wq, bank[4][:, :], ACT.Exp, bias=m0_bc[:, j:j + 1]).then_inc(d_ready, 1)

            act.wait_ge(ctx_md, 1)
            for j in range(8):
                last = A(dc[:, j, :], mdc[:, j, :], ACT.Exp, bias=a_col[:, NL, gate_row(j):gate_row(j) + 1])
            last.then_inc(ctx_d, 1)
            for q in range(8):
                for vb in range(2):
                    act.wait_ge(state_mm, 3 * q + vb + 1)
                    if q >= 1:
                        act.wait_ge(state_stored[vb], 16 * q)
                    A(c_out[vb], bank[4 + vb][:, 0:HD], ACT.Copy).then_inc(state_out, 1)
                act.wait_ge(state_mm, 3 * q + 3)
                if q >= 2:
                    act.wait_ge(n_stored[q % 2], 16 * (q // 2))
                A(n_out[q % 2], bank[6][0:1, 0:HD], ACT.Copy).then_inc(state_out, 1)
            act.wait_ge(ctx_num_mm, 8)
            for q in range(8):
                decay(q)
            for f in (ZO, ZGA, ZGB):
                A(z[:, f:f + 8, :], z[:, f:f + 8, :], ACT.Sigmoid).then_inc(sig_ready, 1)
            for n in range(10):
                act.wait_ge(four_a_mm, n + 1)
                A(four_a[:, n // 2, 2 * (n % 2):2 * (n % 2) + 2].rearrange("p g c f -> p (g c f)"), bank[n % 2][:, :], ACT.Copy).then_inc(four_a_out, 1)
            for g in range(NG):
                act.wait_ge(four_mm, g + 1)
                A(z[:, ZU + g, 0:TL], bank[2 + g % 2][:, :], ACT.Copy)
                A(z[:, ZU + g, TL:T], bank[4 if g % 2 == 0 else 7][:, 0:P], ACT.Copy).then_inc(four_out, 1)
            act.wait_ge(var_ready, 1)
            A(rstd[:, :], rstd[:, :], ACT.Sqrt).then_inc(std_ready, 1)
            for tt in range(NT):
                act.wait_ge(ln_var, tt + 1)
                A(rstd[:, tt:tt + 1], rstd[:, tt:tt + 1], ACT.Sqrt).then_inc(ln_std, 1)
            for tt in range(NT):
                for n in range(2):
                    act.wait_ge(h2_turned, 2 * tt + n + 1)
                    if tt >= 2:
                        act.wait_ge(logits_mm, tt - 1)
                    A(h2T[tt % 2][:, 4 * n:4 * n + 4, :].rearrange("p k t -> p (k t)"), bank[2 + n][:, :], ACT.Copy).then_inc(h2T_ready, 1)
            act.wait_ge(soft_in, 1)
            A(prob[:, :, :], prob[:, :, :], ACT.Exp).then_inc(soft_out, 1)

            def silu(j):
                A(silu_g, bank[0][:, :], ACT.Silu).then_inc(silu_ready, 1)

            def store_y(j, half, s):
                act.wait_ge(down_mm, j + 1)
                A(y_sb[s][:, 0:512], bank[5][:, :], ACT.Copy).then_inc(y_out, 1)
                A(y_sb[s][:, 512:D], bank[6][:, :], ACT.Copy).then_inc(y_out, 1)
                act.wait_ge(y_out, 2 * j + 2)
                act.dma_start(y_d[bass.ds(P * j, P), :], y_sb[s]).then_inc(y_stored[s], 16)

            def split_high(hl, w, full, used, hi, j, used_n=None):
                act.wait_ge(full, 16 * j + 16)
                if used_n is not None:
                    act.wait_ge(used, used_n)
                n = hl.shape[2] // 2
                for b in range(2):
                    A(hl[:, 0, b * n:(b + 1) * n], w[:, b * 2048:(b + 1) * 2048].rearrange("p (k n) -> p k n", k=n), ACT.Copy).then_inc(hi, 1)

            def rows_high(j):
                act.wait_ge(hg_turned, j + 1)
                for n in range(2):
                    A(hgT_hl[:, 0, n * 512:(n + 1) * 512], bank[2 + n][:, :], ACT.Copy).then_inc(rows_hi, 1)

            def aT_high(j):
                act.wait_ge(a_turned, j + 1)
                A(aT_hl[:, 0, :], bank[4][:, :], ACT.Copy).then_inc(aT_hi, 1)

            def step(j, before_half, s):
                act.wait_ge(gate_mm, j + 1)
                act.wait_ge(a_ready, j)
                silu(j)
                aT_high(j - 1)
                split_high(g_hl, g_raw, wg_full, gate_mm, g_hi, j + 1, j + 1)
                rows_high(j + 1)
                split_high(u_hl, u_raw, wu_full, up_mm, u_hi, j + 1, j + 1)
                if not (isinstance(j, int) and j <= 2):
                    act.wait_ge(y_stored[1 - s], 16 * before_half)
                store_y(j - 1, before_half, 1 - s)
                split_high(d_hl, d_raw, wd_full, down_mm, d_hi, j, j)

            half = half_run(act)
            act.wait_ge(y_zeroed, 16)
            split_high(g_hl, g_raw, wg_full, None, g_hi, 0)
            rows_high(0)
            split_high(u_hl, u_raw, wu_full, None, u_hi, 0)
            act.wait_ge(gate_mm, 1)
            silu(0)
            split_high(g_hl, g_raw, wg_full, gate_mm, g_hi, 1, 1)
            rows_high(1)
            split_high(u_hl, u_raw, wu_full, up_mm, u_hi, 1, 1)
            split_high(d_hl, d_raw, wd_full, None, d_hi, 0)
            step(1, 0, 1)
            step(2, 0, 0)
            with act.Fori(1, PAIRS) as i:
                with act.If(i < half):
                    step(2 * i + 1, i, 1)
                    step(2 * i + 2, i, 0)
            aT_high(2 * half)
            act.wait_ge(y_stored[0], 16 * half)
            store_y(2 * half, half, 0)
            for tt in range(NT):
                act.wait_ge(fin_var, tt + 1)
                A(rstd[:, tt:tt + 1], rstd[:, tt:tt + 1], ACT.Sqrt).then_inc(fin_std, 1)

        @block.tensor
        def _(pe):
            MM = nc.tensor.matmul

            def turn(out, in_, rows=P):
                return nc.tensor.transpose(out, in_, ident[0:rows, 0:rows])

            pe.wait_ge(pool_setup, 2)
            pe.wait_ge(stack_loaded, 80)
            turn(bank[7][:, 0:92], stack[:, :], 92).then_inc(stack_turned, 1)
            pe.wait_ge(cond_ready, 1)

            def three(dst, sta, mov, start, stop):
                MM(dst, sta(0), mov(0), start=start, stop=False)
                MM(dst, sta(0), mov(1), start=False, stop=False)
                return MM(dst, sta(1), mov(0), start=False, stop=stop)

            AB = (0, 1, 7)

            def ada_block(n, full, s):
                pe.wait_ge(ada_full[s], 16 * full)
                for k in range(KT):
                    last = MM(bank[AB[s]][0:2, :], cond[:, :].rearrange("p (c k) -> p k c", c=2)[:, k, :], ada_ring[s][:, k, :], start=(k == 0), stop=(k == KT - 1))
                last.then_inc(ada_mm, 1)

            def turn_x(k):
                if k >= 2:
                    pe.wait_ge(h_full, k - 1)
                for tt in range(NL):
                    turn(bank[2 + k % 2][:, tt * P:(tt + 1) * P], x_sb[:, tt, k * P:(k + 1) * P])
                turn(bank[4 + k % 2][:, 0:P], x_sb[:, NL, k * P:(k + 1) * P]).then_inc(x_turned, 1)

            for n in range(ADA_SLOTS):
                ada_block(n, 1, n)
            for n in range(ADA_SLOTS, 2 * ADA_SLOTS):
                pe.wait_ge(mod_ready, n - 2)
                ada_block(n, 2, n - ADA_SLOTS)
            pe.wait_ge(mod_ready, 4)
            for n in range(16):
                last = turn(bank[6][:, 2 * n:2 * n + 2], mod[:, n * P:(n + 1) * P], 2)
            last.then_inc(mod_turned, 1)
            pe.wait_ge(x_loaded, 32)
            for n in range(2 * ADA_SLOTS, N_ADA):
                pe.wait_ge(mod_ready, n - 2)
                ada_block(n, n // ADA_SLOTS + 1, n % ADA_SLOTS)
                if 2 * n - 12 < KT:
                    for k in (2 * n - 12, 2 * n - 11):
                        turn_x(k)
            pe.wait_ge(mod_ready, N_ADA)
            pe.wait_ge(wgate_lo, 1)
            for k in range(KT):
                pe.wait_ge(hT_ready, k + 1)
                hl = (hT_hi, hT_lo)
                for b in range(2):
                    last = three(bank[6 + b][:, 0:TH], lambda n: wgate_hl[:, n, k, :], lambda n: hl[n][:, k, b * TH:(b + 1) * TH], k == 0, k == KT - 1)
            last.then_inc(gates_mm, 1)

            def z_block(b, first=False, third=False):
                hl = (hT_hi, hT_lo)
                for f in range(4):
                    pe.wait_ge(w_lo, 4 * b + f + 1)
                    if not first:
                        pe.wait_ge(z_out, 4 * b + f - 3)
                        pe.wait_ge(z_out2, 4 * b + f - 3)
                    elif f == 3:
                        pe.wait_ge(gates_out, 4)
                    if third and f == 3:
                        pe.wait_ge(gate_cols, 2)
                    for half, done in ((0, z_mm), (1, w_used)):
                        for k in range(KT):
                            last = three(bank[2 * f + half][:, 0:TH], lambda n: w_hl[:, f % 2, n, k, :], lambda n: hl[n][:, k, half * TH:(half + 1) * TH], k == 0, k == KT - 1)
                        last.then_inc(done, 1)

            z_block(0, first=True)
            z_block(1)
            pe.wait_ge(gate_rows, 1)
            pe.wait_ge(z_out, 8)
            pe.wait_ge(z_out2, 8)
            for n in range(2 * NT):
                src = (gate_i, bm_row)[n // NT]
                last = turn(bank[6 + n // NT][:, (n % NT) * GR:(n % NT + 1) * GR], src[:, (n % NT) * P:(n % NT + 1) * P], GR)
            last.then_inc(gate_turned, 1)
            z_block(2, third=True)
            with pe.Fori(3, N_ZB) as i:
                z_block(i)
            pe.wait_ge(z_out, NZ)
            pe.wait_ge(z_out2, NZ)
            for n in range(2 * NT):
                if n >= 4:
                    pe.wait_ge(v_out if n % 2 == 0 else v_out_dve, (n - 4) // 2 + 1)
                for f in range(4):
                    last = turn(bank[n % 4][:, f * P:(f + 1) * P], z[:, ZV + 4 * (n % 2) + f, (n // 2) * P:(n // 2 + 1) * P])
                last.then_inc(v_turned, 1)
            for n in range(2):
                for f in range(4):
                    last = turn(bank[4 + n][:, f * P:(f + 1) * P], z[:, ZK + 4 * n + f, TL:T])
                last.then_inc(k_turned, 1)
            pe.wait_ge(c0_loaded, 16)
            pe.wait_ge(v_out, 5)
            pe.wait_ge(v_out_dve, 5)
            for j in range(8):
                if j >= 4:
                    pe.wait_ge(c0_out, j - 3)
                for kb in range(2):
                    for vb in range(2):
                        last = turn(bank[j % 4][:, (2 * kb + vb) * P:(2 * kb + vb + 1) * P], c0_raw[:, j, vb, kb * P:(kb + 1) * P])
                last.then_inc(c0_turned, 1)
            pe.wait_ge(c0_out, 8)
            pe.wait_ge(n0_out, 1)
            pe.wait_ge(k_out, 2)
            pe.wait_ge(gate_cols, 2)

            def minus_m(dst, j, lo, hi):
                r = gate_row(j)
                return MM(dst, ident[0:GR, r:r + 1].to_broadcast([GR, P]), neg_m[:, lo:hi], start=True, stop=True)

            for h in range(H):
                for b in range(2):
                    MM(bank[0][:, h * P:(h + 1) * P], z[:, ZK + 2 * h + b, TL:T], z[:, ZQ + 2 * h + b, TL:T], start=(b == 0), stop=(b == 1))
            for j in range(8):
                last = minus_m(bank[1 + j // 4][:, (j % 4) * P:(j % 4 + 1) * P], j, TL, T)
            last.then_inc(ctx_mm, 1)
            pe.wait_ge(ctx_p, 1)
            for q in range(8):
                h, d = q // 2, q % 2
                j = d * 4 + h
                if q >= 1:
                    pe.wait_ge(ctx_num_out, q)
                MM(bank[3][:, 0:257], dc[:, j, :], vaug[:, NL, h, :], start=True, stop=True).then_inc(ctx_num_mm, 1)
                for vb in range(2):
                    if q >= 1:
                        pe.wait_ge(state_out, 3 * q - 2 + vb)
                    MM(bank[4 + vb][:, 0:HD], wv[:, j, vb * P:(vb + 1) * P], ktok[:, h * HD:(h + 1) * HD], start=True, stop=True).then_inc(state_mm, 1)
                if q >= 1:
                    pe.wait_ge(state_out, 3 * q)
                MM(bank[6][0:1, 0:HD], w_col[:, j:j + 1], ktok[:, h * HD:(h + 1) * HD], start=True, stop=True).then_inc(state_mm, 1)
            pe.wait_ge(ctx_num_out, 8)
            pe.wait_ge(state_out, 24)

            def scores(h):
                for s in range(NL):
                    for b in range(2):
                        last = MM(bank[s][:, :], z[:, ZK + 2 * h + b, s * P:(s + 1) * P], z[:, ZQ + 2 * h + b, 0:TL], start=(b == 0), stop=(b == 1))
                last.then_inc(s_mm, 1)

            def maxima(q):
                if q >= 1:
                    pe.wait_ge(d_ready, q)
                minus_m(bank[4][:, :], (q % 2) * 4 + q // 2, 0, TL).then_inc(m_mm, 1)

            def units(q):
                h, d = q // 2, q % 2
                j = d * 4 + h
                dec = dp[q % 2]
                for tt in range(NL):
                    u = 4 * q + tt
                    if u >= 3:
                        pe.wait_ge(unit_out, u - 2)
                    dst = bank[5 + u % 3][:, 0:257]
                    for n, s in enumerate(range(tt + 1) if d == 0 else range(tt, NL)):
                        MM(dst, dec[:, s, tt * P:(tt + 1) * P], vaug[:, s, h, :], start=(n == 0), stop=False)
                    for b in range(2):
                        last = MM(dst, qs[q % 2][:, b, tt * P:(tt + 1) * P], c0T[:, j, b, :], start=False, stop=(b == 1))
                    last.then_inc(unit_mm, 1)

            scores(0)
            maxima(0)
            for q in range(8):
                if q + 1 < 8 and q % 2 == 0:
                    maxima(q + 1)
                pe.wait_ge(p_ready, q + 1)
                if q % 2 == 1 and q + 1 < 8:
                    scores(q // 2 + 1)
                    maxima(q + 1)
                units(q)
            pe.wait_ge(unit_out, 32)
            pe.wait_ge(four_loaded, 32)
            for n in range(10):
                if n >= 2:
                    pe.wait_ge(four_a_out, n - 1)
                for g in range(2):
                    last = MM(bank[n % 2][:, g * 256:(g + 1) * 256], z[:, ZU + 2 * (n % 2) + g, (n // 2) * P:(n // 2 + 1) * P], t128_sb[:, 0:256], start=True, stop=True)
                last.then_inc(four_a_mm, 1)
            pe.wait_ge(four_a_out, 10)
            for g in range(NG):
                if g >= 2:
                    pe.wait_ge(four_out, g - 1)
                for s in range(NL):
                    for c in range(2):
                        MM(bank[2 + g % 2][:, :], four_a[:, s, g, c, :], four_l[:, c, s, :], start=(s + c == 0), stop=(s == NL - 1 and c == 1))
                ctx_bank = bank[4 if g % 2 == 0 else 7]
                for c in range(2):
                    last = MM(ctx_bank[:, 0:P], four_a[:, NL, g, c, :], t128_sb[:, 256 * c:256 * c + P], start=(c == 0), stop=(c == 1))
                last.then_inc(four_mm, 1)
            pe.wait_ge(four_out, NG)
            TB = ((6, 7), (4, 5))
            for k in range(KT):
                pe.wait_ge(hn_ready, 1)
                if k >= 2:
                    pe.wait_ge(yin_ready, k - 1)
                for tt in range(NL):
                    last = turn(bank[TB[k % 2][0]][:, tt * P:(tt + 1) * P], hsum[:, tt, k * P:(k + 1) * P])
                last.then_inc(hn_turned, 1)
                turn(bank[TB[k % 2][1]][:, 0:P], hsum[:, NL, k * P:(k + 1) * P]).then_inc(hn_turned, 1)
            pe.wait_ge(wab_loaded, 32)
            YB = ((0, 1, 2), (3, 4, 5))
            for m in range(KT):
                ba, bc, bb = YB[m % 2]
                if m == 0:
                    pe.wait_ge(yin_ready, KT)
                if m >= 2:
                    pe.wait_ge(y_gated, m - 1)
                for w, base, kt, dst, off in ((wa_sb, ZO, KT, ba, 0), (wb_sb, ZU, 4, bb, P)):
                    for k in range(kt):
                        MM(bank[dst][:, :], w[:, k, m * P:(m + 1) * P], z[:, base + k, 0:TL], start=(k == 0), stop=(k == kt - 1))
                    for k in range(kt):
                        last = MM(bank[bc][:, off:off + P], w[:, k, m * P:(m + 1) * P], z[:, base + k, TL:T], start=(k == 0), stop=(k == kt - 1))
                last.then_inc(y_mm, 1)
            pe.wait_ge(wo_loaded, 16)
            OB = ((6, 7), (0, 1))
            pe.wait_ge(merged, KT)
            for tt in range(NT):
                if tt >= 2:
                    pe.wait_ge(o_out, tt - 1)
                for n in range(2):
                    for k in range(KT):
                        last = MM(bank[OB[tt % 2][n]][:, :], z[:, ZGA + k, tt * P:(tt + 1) * P], wo_sb[:, k, n * 512:(n + 1) * 512], start=(k == 0), stop=(k == KT - 1))
                    last.then_inc(o_mm, 1)

            def router(tt):
                for k in range(KT):
                    pe.wait_ge(h2T_ready, 2 * tt + k // 4 + 1)
                    last = MM(bank[4][:, tt * E:(tt + 1) * E], h2T[tt % 2][:, k, :], wr_sb[:, k, :], start=(k == 0), stop=(k == KT - 1))
                last.then_inc(logits_mm, 1)

            for tt in range(NT):
                pe.wait_ge(h2_ready, tt + 1)
                for n in range(2):
                    if tt >= 1:
                        pe.wait_ge(h2T_ready, 2 * tt - 1 + n)
                    for k in range(4):
                        last = turn(bank[2 + n][:, k * P:(k + 1) * P], h2[:, tt, (4 * n + k) * P:(4 * n + k + 1) * P])
                    last.then_inc(h2_turned, 1)
                router(tt)
            pe.wait_ge(chosen, 1)
            for tt in range(NT):
                for s in range(tt):
                    MM(bank[5][:, tt * E:(tt + 1) * E], ones[:, :], rt[:, 5, s, :], start=(s == 0), stop=False)
                MM(bank[5][:, tt * E:(tt + 1) * E], before[:, :], rt[:, 5, tt, :], start=(tt == 0), stop=True)
            for s in range(NT):
                last = MM(bank[5][:, NT * E:(NT + 1) * E], ones[:, :], rt[:, 5, s, :], start=(s == 0), stop=(s == NT - 1))
            last.then_inc(rank_mm, 1)
            pe.wait_ge(table_f, 1)
            turn(bank[7][:, 0:ROW_TILES], slot_rows_f[:, :], ROW_TILES).then_inc(table_turned, 1)

            def turn_rows(j, full, s):
                pe.wait_ge(hg_full[s], 16 * full)
                for n in range(2):
                    for k in range(4):
                        last = turn(bank[2 + n][:, k * P:(k + 1) * P], hg[s][:, (4 * n + k) * P:(4 * n + k + 1) * P])
                last.then_inc(hg_turned, 1)

            def project(dst, hl, lo, j):
                for k in range(KT):
                    if k % 4 == 0:
                        pe.wait_ge(lo, 2 * j + k // 4 + 1)
                    last = three(dst[:, :], lambda n: hgT_hl[:, n, k * P:(k + 1) * P], lambda n: hl[:, n, k, :], k == 0, k == KT - 1)
                return last

            def turn_a():
                for f in range(4):
                    last = turn(bank[4][:, f * P:(f + 1) * P], act_a[:, f * P:(f + 1) * P])
                last.then_inc(a_turned, 1)

            def down(j):
                pe.wait_ge(aT_ready, j + 1)
                pe.wait_ge(d_lo, 2 * j + 2)
                for b in range(2):
                    for f in range(4):
                        last = three(bank[5 + b][:, :], lambda n: aT_hl[:, n, f * P:(f + 1) * P], lambda n: d_hl[:, n, f, b * 512:(b + 1) * 512], f == 0, f == 3)
                last.then_inc(down_mm, 1)

            def moe_step(j, s, full, y_free=True):
                pe.wait_ge(hgT_ready, j + 1)
                pe.wait_ge(silu_ready, j)
                project(bank[0], g_hl, g_lo, j).then_inc(gate_mm, 1)
                pe.wait_ge(a_ready, j)
                turn_a()
                project(bank[1], u_hl, u_lo, j).then_inc(up_mm, 1)
                turn_rows(j + 1, full, 1 - s)
                if y_free:
                    pe.wait_ge(y_out, 2 * j - 2)
                down(j - 1)

            half = half_run(pe)
            turn_rows(0, 1, 0)
            pe.wait_ge(hgT_ready, 1)
            project(bank[0], g_hl, g_lo, 0).then_inc(gate_mm, 1)
            project(bank[1], u_hl, u_lo, 0).then_inc(up_mm, 1)
            turn_rows(1, 1, 1)
            moe_step(1, 1, 2, y_free=False)
            moe_step(2, 0, 2)
            with pe.Fori(1, PAIRS) as i:
                with pe.If(i < half):
                    moe_step(2 * i + 1, 1, i + 2)
                    moe_step(2 * i + 2, 0, i + 2)
            pe.wait_ge(a_ready, 2 * half + 1)
            turn_a()
            pe.wait_ge(y_out, 4 * half)
            down(2 * half)

        @block.vector
        def _(dve):
            V = nc.vector
            chain = [0]

            def then(ins):
                chain[0] += 1
                ins.then_inc(dve_chain, 1)
                dve.wait_ge(dve_chain, chain[0])

            dve.wait_ge(stack_turned, 1)
            V.tensor_copy(cols[:, :], bank[7][:, 0:92]).then_inc(cols_ready, 1)
            dve.wait_ge(pool_setup, 10)
            dve.wait_ge(misc_loaded, 16 * 10)
            V.tensor_copy(wgate[:, :, :].rearrange("p k (g c) -> p k g c", g=4)[:, :, :, 0:4],
                          wgate_raw[:, :, :].rearrange("p k (g c) -> p k g c", g=4)).then_inc(wgate_ready, 1)
            dve.wait_ge(bada_loaded, 16)

            def low(u, f):
                dve.wait_ge(w_hi, u + 1)
                V.tensor_tensor(w_hl[:, f % 2, 1], raw[f // 2][:, :, (f % 2) * P:(f % 2 + 1) * P], w_hl[:, f % 2, 0].bitcast(F32), ALU.subtract).then_inc(w_lo, 1)

            def mod_block(n):
                dve.wait_ge(ada_mm, n + 1)
                V.tensor_tensor(mod[:, n * 512:(n + 1) * 512], bank[(0, 1, 7)[n % 3]][0:2, :], b_ada[:, n * 512:(n + 1) * 512], ALU.add).then_inc(mod_ready, 1)

            for n in range(2 * ADA_SLOTS):
                mod_block(n)
            dve.wait_ge(mod_turned, 1)
            turned = bank[6][:, 0:32].rearrange("p (n c) -> p n c", c=2)
            V.tensor_copy(mcols[:, 0:8, :], turned[:, 0:8, :]).then_inc(dve_chain, 1)
            V.tensor_scalar_add(mcols[:, 8:16, :], turned[:, 8:16, :], 1.0).then_inc(mcols_ready, 1)
            chain[0] += 1
            for n in range(2 * ADA_SLOTS, N_ADA):
                mod_block(n)
                if 2 * n - 12 < KT:
                    for k in (2 * n - 12, 2 * n - 11):
                        dve.wait_ge(h_hi, k + 1)
                        V.tensor_tensor(hT_lo[:, k, :], h_tmp[k % 2], hT_hi[:, k, :].bitcast(F32), ALU.subtract).then_inc(hT_ready, 1)
            dve.wait_ge(wgate_hi, 1)
            V.tensor_tensor(wgate_hl[:, 1], wgate, wgate_hl[:, 0].bitcast(F32), ALU.subtract).then_inc(wgate_lo, 1)
            for f in range(2):
                low(f, f)
            dve.wait_ge(gates_out, 4)
            V.tensor_scalar(gate_i, gate_i, gbias[:, 0:1], None, ALU.add).then_inc(dve_chain, 1)
            V.memset(zero_row, 0.0).then_inc(dve_chain, 1)
            V.memset(b_row, 0.0).then_inc(dve_chain, 1)
            V.memset(m_row, 0.0).then_inc(dve_chain, 1)
            chain[0] += 4
            then(V.tensor_scalar(gate_f, gate_f, gbias[:, 1:2], None, ALU.add))
            V.scalar_tensor_tensor(out=tmp_g, in0=gate_f, scalar=-1.0, in1=gate_f, op0=ALU.mult, op1=ALU.min).then_inc(gate_abs, 1)

            def gate_stage():
                dve.wait_ge(gate_exp, 1)
                then(V.scalar_tensor_tensor(out=log_f, in0=gate_f, scalar=0.0, in1=tmp_g, op0=ALU.min, op1=ALU.subtract))
                spans = []
                for lo, hi in ((0, TL), (TL, T)):
                    spans.append((slice(0, 4), slice(lo, hi), lo))
                    spans.append((slice(32, 36), slice(hi - 1, lo - 1 if lo else None, -1), lo))
                for r, t, lo in spans:
                    last = V.tensor_tensor_scan(b_row[r, t], log_f[r, t], zero_row[r, t], 0.0, ALU.add, ALU.add)
                then(last)
                then(V.tensor_tensor(gate_i, gate_i, b_row, ALU.subtract))
                for r, t, lo in spans:
                    init = m0_col[r, 0:1] if lo == 0 else 0.0
                    last = V.tensor_tensor_scan(m_row[r, t], gate_i[r, t], gate_i[r, t], init, ALU.max, ALU.max)
                then(last)
                then(V.tensor_tensor(bm_row, b_row, m_row, ALU.add))
                V.tensor_scalar_mul(neg_m[:, :], m_row, -1.0).then_inc(gate_rows, 1)

            def z_block(b, last=False):
                for f in range(4):
                    dve.wait_ge(w_used, 4 * b + f + 1)
                    V.tensor_tensor(z[:, bass.ds(4 * b + f, 1), TH:T].rearrange("p a t -> p (a t)"), bank[2 * f + 1][:, 0:TH],
                                    cols[:, bass.ds(16 + 4 * b + f, 1)].to_broadcast([P, TH]), ALU.add).then_inc(z_out2, 1)
                    if not last or f < 2:
                        low(4 * b + f + 2, (f + 2) % 4)

            dve.wait_ge(mod_stored, 16)
            dve.wait_ge(zeros_stored, 16)
            z_block(0)
            gate_stage()
            z_block(1)
            dve.wait_ge(gate_turned, 1)
            V.tensor_copy(a_col[:, :, :], bank[6][:, 0:5 * GR].rearrange("p (t g) -> p t g", t=NT)).then_inc(gate_cols, 1)
            with dve.Fori(2, N_ZB - 2) as i:
                z_block(i)
            dve.wait_ge(small_stored, 32)
            z_block(N_ZB - 2)
            z_block(N_ZB - 1, last=True)
            V.memset(vaug[:, :, :, HD:HD + 1], 1.0).then_inc(dve_chain, 1)
            chain[0] += 1
            for n in range(1, 10, 2):
                dve.wait_ge(v_turned, n + 1)
                V.tensor_copy(vaug[:, n // 2, 2:4, 0:HD], bank[n % 4][:, :].rearrange("p (h v) -> p h v", h=2)).then_inc(v_out_dve, 1)
            V.tensor_copy(c0T[:, :, :, HD:HD + 1], cols[:, 76:92].rearrange("p (j b o) -> p j b o", j=8, b=2)).then_inc(n0_out, 1)

            def masked(q):
                d = q % 2
                dve.wait_ge(m_mm, q + 1)
                V.tensor_tensor(md.rearrange("p (b t) -> p b t", b=NL), bank[4][:, :].rearrange("p (b t) -> p b t", b=NL),
                                mask_neg[:, d, :].unsqueeze(1).to_broadcast([P, NL, P]), ALU.add).then_inc(md_ready, 1)

            def weighted(q):
                h, d = q // 2, q % 2
                dec = dp[q % 2]
                dve.wait_ge(d_ready, q + 1)
                dve.wait_ge(s_mm, h + 1)
                for b in range(2):
                    V.tensor_tensor(qs[q % 2][:, b, :], z[:, ZQ + 2 * h + b, 0:TL], wq, ALU.mult)
                for s in range(NL):
                    lo, hi = (s * P, TL) if d == 0 else (0, (s + 1) * P)
                    last = V.scalar_tensor_tensor(out=dec[:, s, lo:hi], in0=bank[s][:, lo:hi], scalar=HD ** -0.5, in1=dec[:, s, lo:hi], op0=ALU.mult, op1=ALU.mult)
                last.then_inc(p_ready, 1)

            def finish_rows(num, n, tt, h, d, out_sem):
                r = gate_row(d * 4 + h)
                low = den[:, 2 * (n % 2):2 * (n % 2) + 1]
                inv = den[:, 2 * (n % 2) + 1:2 * (n % 2) + 2]
                then(V.tensor_scalar(low, num[:, HD:HD + 1], -1.0, em_col[:, tt, r:r + 1], ALU.mult, ALU.max))
                then(V.tensor_tensor(low, low, num[:, HD:HD + 1], ALU.max))
                then(V.reciprocal(inv, low))
                out = hsum[:, tt, h * HD:(h + 1) * HD]
                if d == 0:
                    V.tensor_scalar(out, num[:, 0:HD], inv, None, ALU.mult).then_inc(out_sem, 1)
                else:
                    V.scalar_tensor_tensor(out=out, in0=num[:, 0:HD], scalar=inv, in1=out, op0=ALU.mult, op1=ALU.add).then_inc(out_sem, 1)

            def consume(q):
                for tt in range(NL):
                    u = 4 * q + tt
                    dve.wait_ge(unit_mm, u + 1)
                    finish_rows(bank[5 + u % 3], u, tt, q // 2, q % 2, unit_out)

            dve.wait_ge(gate_cols, 2)
            dve.wait_ge(ctx_mm, 1)
            for d in range(2):
                last = V.tensor_tensor(mdc[:, 4 * d:4 * d + 4, :], bank[1 + d][:, :].rearrange("p (j t) -> p j t", j=4),
                                       mask_neg[:, d, :].unsqueeze(1).to_broadcast([P, 4, P]), ALU.add)
            last.then_inc(ctx_md, 1)
            dve.wait_ge(ctx_d, 1)
            V.tensor_copy(w_col[:, 0:4], dc[:, 0:4, P - 1])
            then(V.tensor_copy(w_col[:, 4:8], dc[:, 4:8, 0]))
            for j in range(8):
                V.tensor_scalar(wv[:, j, :], vaug[:, NL, j % 4, 0:HD], w_col[:, j:j + 1], None, ALU.mult)
            for d in range(2):
                part = dc[:, 4 * d:4 * d + 4, :]
                last = V.scalar_tensor_tensor(out=part, in0=bank[0][:, :].rearrange("p (j t) -> p j t", j=4), scalar=HD ** -0.5, in1=part, op0=ALU.mult, op1=ALU.mult)
            last.then_inc(ctx_p, 1)
            for q in range(8):
                dve.wait_ge(ctx_num_mm, q + 1)
                finish_rows(bank[3], q, NL, q // 2, q % 2, ctx_num_out)
            masked(0)
            weighted(0)
            for q in range(8):
                if q + 1 < 8:
                    masked(q + 1)
                consume(q)
                if q + 1 < 8:
                    weighted(q + 1)
            dve.wait_ge(unit_out, 32)
            for n in range(20):
                last = V.bn_stats(bn[:, n, :], hsum[:, n // 4, (n % 4) * HD:(n % 4 + 1) * HD])
            then(last)
            for n in range(20):
                last = V.bn_aggr(mv[:, n, :], bn[:, n, :])
            then(last)
            V.tensor_scalar_add(rstd[:, :], mv[:, :, 1], EPS).then_inc(var_ready, 1)
            dve.wait_ge(std_ready, 1)
            then(V.reciprocal(rstd[:, :], rstd[:, :]))
            for n in range(20):
                v = hsum[:, n // 4, (n % 4) * HD:(n % 4 + 1) * HD]
                last = V.tensor_scalar(v, v, mv[:, n, 0:1], rstd[:, n:n + 1], ALU.subtract, ALU.mult)
            last.then_inc(hn_ready, 1)
            dve.wait_ge(sig_ready, 3)
            TB = ((6, 7), (4, 5))
            for k in range(KT):
                for (lo, hi), b, c in (((0, TL), 0, 1), ((TL, T), 1, 2)):
                    dve.wait_ge(hn_turned, 2 * k + c)
                    last = V.scalar_tensor_tensor(out=z[:, ZO + k, lo:hi], in0=bank[TB[k % 2][b]][:, 0:hi - lo], scalar=cols[:, 68 + k:69 + k],
                                                  in1=z[:, ZO + k, lo:hi], op0=ALU.mult, op1=ALU.mult)
                last.then_inc(yin_ready, 1)
            YB = ((0, 1, 2), (3, 4, 5))
            for m in range(KT):
                ba, bc, bb = YB[m % 2]
                dve.wait_ge(y_mm, m + 1)
                for base, latent, off in ((ZGA, ba, 0), (ZGB, bb, P)):
                    V.tensor_tensor(z[:, base + m, 0:TL], z[:, base + m, 0:TL], bank[latent][:, :], ALU.mult)
                    last = V.tensor_tensor(z[:, base + m, TL:T], z[:, base + m, TL:T], bank[bc][:, off:off + P], ALU.mult)
                last.then_inc(y_gated, 1)
            dve.wait_ge(rows1_loaded, 16 * 8)
            V.tensor_scalar_add(rows1[:, S2L:S2C + 1, :], rows1[:, S2L:S2C + 1, :], 1.0).then_inc(rows1_ready, 1)
            dve.wait_ge(xr_loaded, 32)

            def norm_in(tt, row, var_sem, std_sem, seen):
                for n in range(2):
                    last = V.bn_stats(bn[:, n, :], row[:, n * 512:(n + 1) * 512])
                then(last)
                then(V.bn_aggr(mv[:, tt, :], bn[:, 0:2, :]))
                V.tensor_scalar_add(rstd[:, tt:tt + 1], mv[:, tt, 1:2], EPS).then_inc(var_sem, 1)
                dve.wait_ge(std_sem, seen)
                then(V.reciprocal(rstd[:, tt:tt + 1], rstd[:, tt:tt + 1]))
                return V.tensor_scalar(row, row, mv[:, tt, 0:1], rstd[:, tt:tt + 1], ALU.subtract, ALU.mult)

            OB = ((6, 7), (0, 1))
            for tt in range(NT):
                c = 0 if tt < NL else 1
                for n in range(2):
                    dve.wait_ge(o_mm, 2 * tt + n + 1)
                    o = bank[OB[tt % 2][n]]
                    V.tensor_tensor(o[:, :], o[:, :], rows1[:, G1L + c, n * 512:(n + 1) * 512], ALU.mult).then_inc(dve_chain, 1)
                    chain[0] += 1
                dve.wait_ge(dve_chain, chain[0])
                for n in range(2):
                    o = bank[OB[tt % 2][n]]
                    row = xr[:, tt, n * 512:(n + 1) * 512]
                    last = V.scalar_tensor_tensor(out=row, in0=row, scalar=ALPHA, in1=o[:, :], op0=ALU.mult, op1=ALU.add)
                last.then_inc(o_out, 1)
                dve.wait_ge(o_out, tt + 1)
                norm_in(tt, xr[:, tt, :], ln_var, ln_std, tt + 1).then_inc(xn_ready, 1)
            dve.wait_ge(logits_mm, NT)
            dve.wait_ge(misc_loaded, 16 * 10)
            then(V.tensor_tensor(prob[:, :, :], bank[4][:, 0:NT * E].rearrange("p (t e) -> p t e", t=NT),
                                 br_bc[:, :].unsqueeze(1).to_broadcast([P, NT, E]), ALU.add))
            then(V.tensor_reduce(rs[:, 0, 0:NT], prob[:, :, :], AX, ALU.max))
            V.tensor_tensor(prob[:, :, :], prob[:, :, :], rs[:, 0, 0:NT].unsqueeze(2).to_broadcast([P, NT, E]), ALU.subtract).then_inc(soft_in, 1)
            dve.wait_ge(soft_out, 1)
            then(V.tensor_reduce(rs[:, 0, 0:NT], prob[:, :, :], AX, ALU.add))
            then(V.reciprocal(rs[:, 0, 0:NT], rs[:, 0, 0:NT]))
            then(V.tensor_tensor(prob[:, :, :], prob[:, :, :], rs[:, 0, 0:NT].unsqueeze(2).to_broadcast([P, NT, E]), ALU.mult))

            def wide(n):
                return rs[:, n, :].unsqueeze(2).to_broadcast([P, NT * EG, EPG])

            def groups(t):
                return t.rearrange("p t (g e) -> p (t g) e", g=EG)

            rev = rev4[:, :].unsqueeze(1).to_broadcast([P, NT * EG, EPG])
            pg = groups(prob[:, :, :])
            R = [groups(rt[:, n]) for n in range(6)]

            def first_max(values, top, mask, key):
                then(V.tensor_reduce(rs[:, top, :], values, AX, ALU.max))
                then(V.tensor_tensor(mask, values, wide(top), ALU.is_equal))
                then(V.tensor_tensor(mask, mask, rev, ALU.mult))
                then(V.tensor_reduce(rs[:, key, :], mask, AX, ALU.max))
                then(V.tensor_tensor(mask, mask, wide(key), ALU.is_equal))

            first_max(pg, 0, R[0], 1)
            then(V.scalar_tensor_tensor(out=R[1], in0=R[0], scalar=-2.0, in1=pg, op0=ALU.mult, op1=ALU.add))
            first_max(R[1], 2, R[2], 3)
            then(V.tensor_tensor(rs[:, 4, :], rs[:, 0, :], rs[:, 2, :], ALU.add))
            by_group = rs[:, 4, :].rearrange("p (t g) -> p t g", g=EG)
            mask_g = rs[:, 6, :].rearrange("p (t g) -> p t g", g=EG)
            rev_g = rev4[:, :].unsqueeze(1).to_broadcast([P, NT, EG])
            top_bc = rs[:, 5, 0:NT].unsqueeze(2).to_broadcast([P, NT, EG])
            then(V.tensor_reduce(rs[:, 5, 0:NT], by_group, AX, ALU.max))
            then(V.tensor_tensor(mask_g, by_group, top_bc, ALU.is_equal))
            then(V.tensor_tensor(mask_g, mask_g, rev_g, ALU.mult))
            then(V.tensor_reduce(rs[:, 5, 0:NT], mask_g, AX, ALU.max))
            then(V.tensor_tensor(mask_g, mask_g, top_bc, ALU.is_equal))
            then(V.reciprocal(rs[:, 7, :], rs[:, 4, :]))
            then(V.tensor_tensor(rs[:, 7, :], rs[:, 7, :], rs[:, 6, :], ALU.mult))
            for k, top in enumerate((0, 2)):
                then(V.tensor_tensor(rs[:, 8 + k, :], rs[:, top, :], rs[:, 7, :], ALU.mult))
                then(V.tensor_reduce(wtok[:, k, :], rs[:, 8 + k, :].rearrange("p (t g) -> p t g", g=EG), AX, ALU.add))
            then(V.tensor_tensor(R[0], R[0], wide(6), ALU.mult))
            then(V.tensor_tensor(R[2], R[2], wide(6), ALU.mult))
            V.tensor_tensor(R[5], R[0], R[2], ALU.add).then_inc(chosen, 1)
            dve.wait_ge(rank_mm, 1)
            cnt = bank[5][:, NT * E:(NT + 1) * E]
            then(V.tensor_tensor(cnt5[:, :, :], cnt.unsqueeze(2).to_broadcast([P, E, NT]), thresh[:, :].unsqueeze(1).to_broadcast([P, E, NT]), ALU.is_gt))
            then(V.tensor_reduce(est[:, 0, :], cnt5[:, :, :], AX, ALU.add))
            then(V.memset(est[:, 3, :], 0.0))
            then(V.tensor_tensor_scan(est[:, 1, :], est[:, 0, :], est[:, 3, :], 0.0, ALU.add, ALU.add))
            then(V.tensor_tensor(est[:, 2, :], est[:, 1, :], est[:, 0, :], ALU.subtract))
            then(V.tensor_scalar_mul(est[:, 2, :], est[:, 2, :], float(P)))
            then(V.tensor_tensor(rt[:, 3], bank[5][:, 0:NT * E].rearrange("p (t e) -> p t e", t=NT), est[:, 2, :].unsqueeze(1).to_broadcast([P, NT, E]), ALU.add))
            for k, n in enumerate((0, 2)):
                then(V.tensor_tensor(rt[:, 4], rt[:, 3], rt[:, n], ALU.mult))
                then(V.tensor_reduce(slot_f[:, k, :], rt[:, 4], AX, ALU.add))
            then(V.tensor_copy(slot_i[:, :], slot_f[:, :, :].rearrange("p k t -> p (k t)")))
            then(V.tensor_tensor(own[:, :, :], est[0:1, 1, :].unsqueeze(1).to_broadcast([1, ROW_TILES, E]),
                                 tile_no[:, :].unsqueeze(2).to_broadcast([1, ROW_TILES, E]), ALU.is_le))
            then(V.tensor_reduce(own_f[:, :], own[:, :, :], AX, ALU.add))
            then(V.tensor_scalar_min(own_f[:, :], own_f[:, :], float(E - 1)))
            then(V.tensor_copy(tile_expert[:, :], own_f[:, :]))
            then(V.tensor_copy(n_tiles[:, :], est[0:1, 1, E - 1:E]))
            V.tensor_scalar(half_tiles[:, :], n_tiles[:, :], 1, None, ALU.arith_shift_right).then_inc(slots_ready, 1)
            dve.wait_ge(table_loaded, 16)
            V.tensor_copy(slot_rows_f[:, :], slot_rows[:, :]).then_inc(table_f, 1)
            dve.wait_ge(table_turned, 1)
            V.tensor_copy(slot_tok[:, :], bank[7][:, 0:ROW_TILES]).then_inc(table_ready, 1)

            def split_low(hl, w, hi, lo, j):
                n = hl.shape[2] // 2
                for b in range(2):
                    dve.wait_ge(hi, 2 * j + b + 1)
                    V.tensor_tensor(hl[:, 1, b * n:(b + 1) * n], w[:, b * 2048:(b + 1) * 2048].rearrange("p (k n) -> p k n", k=n),
                                    hl[:, 0, b * n:(b + 1) * n].bitcast(F32), ALU.subtract).then_inc(lo, 1)

            def rows_low(j):
                for n in range(2):
                    dve.wait_ge(rows_hi, 2 * j + 2)
                    last = V.tensor_tensor(hgT_hl[:, 1, n * 512:(n + 1) * 512], bank[2 + n][:, :], hgT_hl[:, 0, n * 512:(n + 1) * 512].bitcast(F32), ALU.subtract)
                last.then_inc(hgT_ready, 1)

            def product(j):
                dve.wait_ge(silu_ready, j + 1)
                dve.wait_ge(up_mm, j + 1)
                V.tensor_tensor(act_a, silu_g, bank[1][:, :], ALU.mult).then_inc(a_ready, 1)

            def aT_low(j):
                dve.wait_ge(aT_hi, j + 1)
                V.tensor_tensor(aT_hl[:, 1, :], bank[4][:, :], aT_hl[:, 0, :].bitcast(F32), ALU.subtract).then_inc(aT_ready, 1)

            def step(j):
                aT_low(j - 1)
                split_low(g_hl, g_raw, g_hi, g_lo, j + 1)
                product(j)
                rows_low(j + 1)
                split_low(u_hl, u_raw, u_hi, u_lo, j + 1)
                split_low(d_hl, d_raw, d_hi, d_lo, j)

            half = half_run(dve)
            split_low(g_hl, g_raw, g_hi, g_lo, 0)
            rows_low(0)
            split_low(u_hl, u_raw, u_hi, u_lo, 0)
            product(0)
            split_low(g_hl, g_raw, g_hi, g_lo, 1)
            rows_low(1)
            split_low(u_hl, u_raw, u_hi, u_lo, 1)
            split_low(d_hl, d_raw, d_hi, d_lo, 0)
            step(1)
            step(2)
            with dve.Fori(1, PAIRS) as i:
                with dve.If(i < half):
                    step(2 * i + 1)
                    step(2 * i + 2)
            aT_low(2 * half)
            dve.wait_ge(rows2_loaded, 64)
            for tt in range(NT):
                c = 0 if tt < NL else 1
                y0, y1 = yg[tt % 2]
                dve.wait_ge(yg_loaded[tt % 2], 32 * (tt // 2 + 1))
                then(V.tensor_scalar(y0, y0, wtok[:, 0, tt:tt + 1], None, ALU.mult))
                then(V.scalar_tensor_tensor(out=y0, in0=y1, scalar=wtok[:, 1, tt:tt + 1], in1=y0, op0=ALU.mult, op1=ALU.add))
                then(V.tensor_tensor(y0, y0, rows2[:, G2L + c, :], ALU.mult))
                then(V.scalar_tensor_tensor(out=y0, in0=xr[:, tt, :], scalar=ALPHA, in1=y0, op0=ALU.mult, op1=ALU.add))
                then(norm_in(tt, y0, fin_var, fin_std, tt + 1))
                then(V.tensor_tensor(y0, y0, rows2[:, LN2G, :], ALU.mult))
                V.tensor_tensor(y0, y0, rows2[:, LN2B, :], ALU.add).then_inc(out_ready, 1)


_INS = ["x_prompt", "x_sample", "state_C", "state_n", "state_m", "c", "c_ctx", "w_in", "b_in", "w_a", "w_b", "w_out",
        "g_head", "ln1_g", "ln1_b", "ln2_g", "ln2_b", "w_ada", "b_ada", "w_router", "b_router", "w_gate", "w_up", "w_down"]
_OUTS = [("y_prompt", (1, TC, D)), ("y_sample", (1, TL, D)), ("new_C", (1, 1, 2, H, HD, HD)), ("new_n", (1, 1, 2, H, HD)),
         ("new_m", (1, 1, 2, H))]


def kernel(**inputs):
    import concourse.bacc as _bacc
    from concourse.bass_utils import run_bass_kernel_spmd as _run

    nc = _bacc.Bacc("TRN2", target_bir_lowering=False, num_devices=1, dynamic_dma_scratch_size=8192)
    arrays = {n: np.ascontiguousarray(inputs[n]) for n in _INS}
    arrays["t128"], arrays["t512"] = dft_tables()
    args = {n: nc.dram_tensor(n, v.shape, F32, kind="ExternalInput").ap() for n, v in arrays.items()}
    for n, shape in _OUTS:
        args[n] = nc.dram_tensor(n, shape, F32, kind="ExternalOutput").ap()
    build(nc, args)
    r = _run(nc, [arrays], core_ids=[0])
    return tuple(r.results[0][n] for n, _ in _OUTS)
```
